# Optimizing a Trainium2 kernel written in Bass

```python
import jax, jax.numpy as jnp
from jax import lax
import numpy as np

D_MODEL = 1024
BATCH = 1
SEQ = 256
DEPTH = 2

N_MIXERS = 2
N_POOL_LAYERS = (DEPTH + 1) // 2
N_MOBA_LAYERS = DEPTH // 2
POOL_WINDOWS = (2, 4, 8, 16)
N_POOL_GROUPS = len(POOL_WINDOWS)
POOL_GROUP_DIM = D_MODEL // N_POOL_GROUPS
N_HEADS = 16
HEAD_DIM = D_MODEL // N_HEADS
MOBA_BLOCK = 256
MOBA_TOPK = 3
Q_CHUNK = 32
N_EXPERT_GROUPS = 4
EXPERTS_PER_GROUP = 8
N_EXPERTS = N_EXPERT_GROUPS * EXPERTS_PER_GROUP
EXPERT_TOPK = 2
D_EXPERT = D_MODEL // 4
RMS_EPS = 1e-6

kernel_name = "hybrid_pool_moba_hmoe_adaln"

def rmsnorm(x, g):
    xf = x.astype(jnp.float32)
    r = lax.rsqrt(jnp.mean(xf * xf, axis=-1, keepdims=True) + RMS_EPS)
    return (xf * r).astype(x.dtype) * g

def alibi_slopes(n_heads):
    return 2.0 ** (-8.0 * jnp.arange(1, n_heads + 1, dtype=jnp.float32) / n_heads)

def pool_mixer(h, w_pool, pool_scale):
    B, S, D = h.shape
    hf = h.astype(jnp.float32)
    pos = jnp.arange(S)
    outs = []
    for g, w in enumerate(POOL_WINDOWS):
        hg = hf[..., g * POOL_GROUP_DIM:(g + 1) * POOL_GROUP_DIM]
        cs = lax.cumsum(hg, axis=1)
        prev = jnp.pad(cs, ((0, 0), (w, 0), (0, 0)))[:, :S]
        cnt = jnp.minimum(pos + 1, w).astype(jnp.float32)[None, :, None]
        outs.append((cs - prev) / cnt - hg)
    p = jnp.stack(outs, axis=2).astype(h.dtype)
    y = jnp.einsum('bsgc,gcd->bsgd', p, w_pool).reshape(B, S, D)
    return y * pool_scale

def moba_attention(h, w_qkv, w_o):
    B, S, D = h.shape
    H, Dh, BLK, QC = N_HEADS, HEAD_DIM, MOBA_BLOCK, Q_CHUNK
    qkv = h @ w_qkv
    q, k, v = jnp.split(qkv, 3, axis=-1)
    to_heads = lambda t: t.reshape(B, S, H, Dh).transpose(0, 2, 1, 3)
    q, k, v = to_heads(q), to_heads(k), to_heads(v)
    NB = -(-S // BLK)
    K = min(MOBA_TOPK, NB)
    S_pad = NB * BLK
    pad = ((0, 0), (0, 0), (0, S_pad - S), (0, 0))
    q, k, v = jnp.pad(q, pad), jnp.pad(k, pad), jnp.pad(v, pad)
    kb = k.reshape(B, H, NB, BLK, Dh)
    vb = v.reshape(B, H, NB, BLK, Dh)
    kmean = jnp.mean(kb.astype(jnp.float32), axis=3)
    slopes = alibi_slopes(H)
    scale = Dh ** -0.5
    n_chunks = S_pad // QC
    qc_all = q.reshape(B, H, n_chunks, QC, Dh).transpose(2, 0, 1, 3, 4)
    b_idx = jnp.arange(B)[:, None, None, None]
    h_idx = jnp.arange(H)[None, :, None, None]
    blk_ar = jnp.arange(BLK)

    def one_chunk(args):
        ci, q_c = args
        q_pos = ci * QC + jnp.arange(QC)
        own = (ci * QC) // BLK
        gate = jnp.einsum('bhqd,bhnd->bhqn', q_c.astype(jnp.float32), kmean)
        gate = jnp.where(jnp.arange(NB) < own, gate, -jnp.inf)
        _, sel = lax.top_k(gate, K)
        sel_valid = sel < own
        ks = kb[b_idx, h_idx, sel]
        vs = vb[b_idx, h_idx, sel]
        s_sel = jnp.einsum('bhqd,bhqkld->bhqkl', q_c, ks,
                           preferred_element_type=jnp.float32) * scale
        k_pos_sel = sel[..., None] * BLK + blk_ar
        dist_sel = (q_pos[None, None, :, None, None] - k_pos_sel).astype(jnp.float32)
        s_sel = s_sel - slopes[None, :, None, None, None] * dist_sel
        s_sel = jnp.where(sel_valid[..., None], s_sel, -jnp.inf).reshape(B, H, QC, K * BLK)
        k_own = lax.dynamic_slice_in_dim(kb, own, 1, axis=2)[:, :, 0]
        v_own = lax.dynamic_slice_in_dim(vb, own, 1, axis=2)[:, :, 0]
        s_own = jnp.einsum('bhqd,bhld->bhql', q_c, k_own,
                           preferred_element_type=jnp.float32) * scale
        dist_own = (q_pos[:, None] - (own * BLK + blk_ar)[None, :]).astype(jnp.float32)
        s_own = jnp.where(dist_own >= 0, s_own - slopes[None, :, None, None] * dist_own, -jnp.inf)
        p = jax.nn.softmax(jnp.concatenate([s_sel, s_own], axis=-1), axis=-1).astype(q_c.dtype)
        p_sel = p[..., :K * BLK].reshape(B, H, QC, K, BLK)
        p_own = p[..., K * BLK:]
        return (jnp.einsum('bhqkl,bhqkld->bhqd', p_sel, vs)
                + jnp.einsum('bhql,bhld->bhqd', p_own, v_own))

    o = lax.map(one_chunk, (jnp.arange(n_chunks), qc_all))
    o = o.transpose(1, 0, 3, 2, 4).reshape(B, S_pad, D)[:, :S]
    return o @ w_o

def hier_moe(h, w_group, w_expert, w_gate, w_up, w_down):
    B, S, D = h.shape
    t = h.reshape(-1, D)
    T = t.shape[0]
    g_prob = jax.nn.softmax((t @ w_group).astype(jnp.float32), axis=-1)
    g_w, g_sel = lax.top_k(g_prob, 1)
    e_logits = (t @ w_expert).astype(jnp.float32).reshape(T, N_EXPERT_GROUPS, EXPERTS_PER_GROUP)
    e_logits = e_logits[jnp.arange(T), g_sel[:, 0]]
    e_val, e_sel = lax.top_k(e_logits, EXPERT_TOPK)
    e_w = jax.nn.softmax(e_val, axis=-1) * g_w
    expert_id = g_sel * EXPERTS_PER_GROUP + e_sel
    combine = jnp.einsum('tke,tk->te', jax.nn.one_hot(expert_id, N_EXPERTS, dtype=jnp.float32),
                         e_w).astype(t.dtype)
    y = jnp.zeros_like(t)
    for e in range(N_EXPERTS):
        he = jax.nn.silu(t @ w_gate[e]) * (t @ w_up[e])
        y = y + combine[:, e, None] * (he @ w_down[e])
    return y.reshape(B, S, D)

def setup_inputs(seed: int = 0) -> dict:
    key = jax.random.key(seed)
    ks = jax.random.split(key, 20)
    D, F, E, G = D_MODEL, D_EXPERT, N_EXPERTS, N_EXPERT_GROUPS
    nrm = lambda k, shape, s: jax.random.normal(k, shape, jnp.float32) * s
    return {
        "x": nrm(ks[0], (BATCH, SEQ, D), 1.0),
        "c": nrm(ks[1], (BATCH, D), 1.0),
        "ada_w": nrm(ks[2], (DEPTH, D, 6 * D), D ** -0.5),
        "ada_b": nrm(ks[3], (DEPTH, 6 * D), 0.02),
        "norm_mix_g": 1.0 + nrm(ks[4], (DEPTH, D), 0.05),
        "norm_ffn_g": 1.0 + nrm(ks[5], (DEPTH, D), 0.05),
        "pool_w": nrm(ks[6], (N_POOL_LAYERS, N_POOL_GROUPS, POOL_GROUP_DIM, POOL_GROUP_DIM), POOL_GROUP_DIM ** -0.5),
        "pool_scale": 1.0 + nrm(ks[7], (N_POOL_LAYERS, D), 0.1),
        "w_qkv": nrm(ks[8], (N_MOBA_LAYERS, D, 3 * D), D ** -0.5),
        "w_o": nrm(ks[9], (N_MOBA_LAYERS, D, D), D ** -0.5),
        "router_group_w": nrm(ks[10], (DEPTH, D, G), D ** -0.5),
        "router_expert_w": nrm(ks[11], (DEPTH, D, E), D ** -0.5),
        "exp_w_gate": nrm(ks[12], (DEPTH, E, D, F), D ** -0.5),
        "exp_w_up": nrm(ks[13], (DEPTH, E, D, F), D ** -0.5),
        "exp_w_down": nrm(ks[14], (DEPTH, E, F, D), F ** -0.5),
        "final_norm_g": 1.0 + nrm(ks[15], (D,), 0.05),
    }

def reference(x, c, ada_w, ada_b, norm_mix_g, norm_ffn_g, pool_w, pool_scale, w_qkv, w_o,
              router_group_w, router_expert_w, exp_w_gate, exp_w_up, exp_w_down, final_norm_g):
    c_act = jax.nn.silu(c)
    for i in range(DEPTH):
        mod = c_act @ ada_w[i] + ada_b[i]
        sh_m, sc_m, g_m, sh_f, sc_f, g_f = [m[:, None, :] for m in jnp.split(mod, 6, axis=-1)]
        h = rmsnorm(x, norm_mix_g[i]) * (1.0 + sc_m) + sh_m
        if i % N_MIXERS == 0:
            y = pool_mixer(h, pool_w[i // N_MIXERS], pool_scale[i // N_MIXERS])
        else:
            y = moba_attention(h, w_qkv[i // N_MIXERS], w_o[i // N_MIXERS])
        x = x + g_m * y
        h = rmsnorm(x, norm_ffn_g[i]) * (1.0 + sc_f) + sh_f
        x = x + g_f * hier_moe(h, router_group_w[i], router_expert_w[i],
                               exp_w_gate[i], exp_w_up[i], exp_w_down[i])
    return rmsnorm(x, final_norm_g)


_drawn_inputs = setup_inputs


def setup_inputs(seed=0):
    import zlib

    import numpy as np

    out = dict(_drawn_inputs(seed))
    spreads = {}
    factors = {}
    for name, (base, spread) in spreads.items():
        noise = np.random.default_rng([zlib.crc32(name.encode()), seed]).standard_normal(out[name].shape)
        drawn = base * np.exp(spread * noise) if base else spread * noise
        out[name] = __import__('jax').numpy.asarray(drawn.astype(out[name].dtype))
    for name, factor in factors.items():
        out[name] = (out[name] * factor).astype(out[name].dtype)
    return out
```

```python
from contextlib import ExitStack

import numpy as np

import concourse.bass as bass
from concourse import mybir

P = 128
SEQ, D, F, E = 256, 1024, 256, 32
NG, EPG, TOPK = 4, 8, 2
NH, DH = 16, 64
T = SEQ // P
KC = D // P
NSLOT = SEQ * TOPK
SB = NSLOT // P
CAP = 64
PAD = NSLOT + CAP
MAXOVF = NSLOT // CAP - 1
R = 4
SLOT = 3 * D * F // P
AC = SLOT // KC
WINDOWS = (2, 4, 8, 16)
EPS = 1e-6
BIG = 3.0e38
MASKED = -1.0e30

ALU = mybir.AluOpType
ACT = mybir.ActivationFunctionType
F32 = mybir.dt.float32
I32 = mybir.dt.int32
AX = mybir.AxisListType.X

IT_ADA = [0, 1, 2, 3, 5, 6, 7, 8] + [37, 38, 39, 40, 49, 50, 51, 52]
IT_POOL = 4
HEAD_E = 28
IT_EXP = [lambda e: 9 + e if isinstance(e, int) and e < HEAD_E else 41 + e - HEAD_E, lambda e: 55 + e]
IT_QKV = [45, 46, 47, 48]
IT_WO = [53, 54]

ROW_B = [0, 6]
ROW_MIX, ROW_FFN, ROW_PS, ROW_FIN = 12, 14, 16, 17
NROWS = 18


def constants():
    ident = np.eye(P, dtype=np.float32)
    tri = np.triu(np.ones((P, P), np.float32), 1)
    iota = np.broadcast_to(np.arange(NSLOT, dtype=np.float32), (P, NSLOT)).copy()
    pos = np.arange(SEQ)
    band = np.zeros((SEQ, len(WINDOWS), SEQ), np.float32)
    for g, w in enumerate(WINDOWS):
        inside = (pos[:, None] <= pos[None, :]) & (pos[:, None] > pos[None, :] - w)
        band[:, g] = inside / np.minimum(pos + 1, w)[None, :] - np.eye(SEQ)
    band = np.ascontiguousarray(band.reshape(T, P, -1).transpose(1, 0, 2).reshape(P, -1).astype(np.float32))
    dist = pos[:, None] - pos[None, :]
    alibi = np.where(dist >= 0, -dist, MASKED).astype(np.float32)
    alibi = np.concatenate([alibi[:P, :P], alibi[P:, :]], 1)
    slopes = np.broadcast_to((2.0 ** (-8.0 * np.arange(1, NH + 1) / NH)).astype(np.float32), (P, NH)).copy()
    first8 = np.broadcast_to(np.arange(EPG, 0, -1, dtype=np.float32), (P, EPG)).copy()
    misc = np.concatenate([ident, tri, iota, alibi, slopes, first8], 1)
    return {"misc": np.ascontiguousarray(misc), "band": band}


def program(nc, x, c, ada_w, ada_b, norm_mix_g, norm_ffn_g, pool_w, pool_scale, w_qkv, w_o,
            router_group_w, router_expert_w, exp_w_gate, exp_w_up, exp_w_down, final_norm_g, misc, band, out):
    ctx = ExitStack()
    with ctx:
        def sb(name, shape, dt=F32):
            return ctx.enter_context(nc.sbuf_tensor(name, shape, dt))

        sems = {}

        def S(*name):
            key = "_".join(map(str, name))
            if key not in sems:
                sems[key] = ctx.enter_context(nc.semaphore(key))
            return sems[key]

        x_sb = sb("x_sb", [P, T, D])
        mod = sb("mod", [P, 6 * D])
        NM = 2 * P + NSLOT + 3 * P + NH + EPG
        cst = sb("cst", [P, NM])
        ident, tri = cst[:, 0:P], cst[:, P:2 * P]
        iota = cst[:, 2 * P:2 * P + NSLOT]
        o = 2 * P + NSLOT
        alibi, slopes, first8 = cst[:, o:o + 3 * P], cst[:, o + 3 * P:o + 3 * P + NH], cst[:, o + 3 * P + NH:NM]
        ones = sb("ones", [P, P])
        rows = sb("rows", [NROWS, D])
        ccol = sb("ccol", [P, KC])
        cact = sb("cact", [P, KC])
        acc = sb("acc", [P, 2, AC])
        ring = sb("ring", [P, R, SLOT])
        rw = sb("rw", [P, 2, KC, NG + E])
        reg_h = sb("reg_h", [P, T * D])
        reg_a = sb("reg_a", [P, KC * PAD])
        reg_b = sb("reg_b", [P, KC * PAD])
        reg_c = sb("reg_c", [P, 15 * P])

        h = reg_h[:, :].rearrange("p (t d) -> p t d", t=T)
        h_str = reg_h[:, :].rearrange("p (t q k) -> p t k q", t=T, k=KC)
        oT = reg_h[:, :].rearrange("p (m q) -> p m q", m=KC)
        hT = reg_b[:, 0:KC * SEQ].rearrange("p (k q) -> p k q", k=KC)
        band_sb = reg_a[:, 0:T * NG * SEQ].rearrange("p (t g q) -> p t g q", t=T, g=NG)
        pT = reg_a[:, 2048:2048 + KC * SEQ].rearrange("p (m q) -> p m q", m=KC)
        hS = reg_a[:, :].rearrange("p (k s) -> p k s", k=KC)
        yS = reg_a[:, 0:SB * D].rearrange("p (s d) -> p s d", s=SB)
        yT = reg_b[:, :].rearrange("p (m s) -> p m s", m=KC)
        pick = reg_b[:, 2048:2048 + T * NSLOT].rearrange("p (t s) -> p t s", t=T)
        pickw = reg_b[:, 3072:3072 + T * NSLOT].rearrange("p (t s) -> p t s", t=T)
        pwT = reg_c[:, 0:SB * SEQ].rearrange("p (s q) -> p s q", s=SB)
        stage_g = reg_c[:, 0:2 * KC * NG].rearrange("p (l k n) -> p l k n", l=2, k=KC)
        stage_e = reg_c[:, 64:64 + 2 * KC * E].rearrange("p (l k n) -> p l k n", l=2, k=KC)
        qT = reg_a[:, 0:2048].rearrange("p (m q) -> p m q", m=KC)
        kT = reg_a[:, 2048:4096].rearrange("p (m q) -> p m q", m=KC)
        v = reg_b[:, 2048:4096].rearrange("p (t d) -> p t d", t=T)
        sc = [reg_c[:, 3 * P * b:3 * P * (b + 1)] for b in range(2)]
        pr = [reg_c[:, 3 * P * (2 + b):3 * P * (3 + b)] for b in range(2)]
        prT = [reg_c[:, 12 * P:15 * P], reg_b[:, 4096:4096 + 3 * P]]

        ss = sb("ss", [P, T])
        ms = sb("ms", [P, T])
        rt = sb("rt", [P, T])
        rs = sb("rs", [P, T])
        nmx = sb("nmx", [P, 2, T])
        psm = sb("psm", [P, 2, T])
        prc = sb("prc", [P, 2, T])
        sil = sb("sil", [P, 2, 2 * CAP])
        he = sb("he", [P, 2, 2 * CAP])
        lg = sb("lg", [P, T, NG + E])
        gm = sb("gm", [P, T, 1])
        gd = sb("gd", [P, T, NG])
        gsum = sb("gsum", [P, T, 1])
        gw = sb("gw", [P, T, 1])
        geq = sb("geq", [P, T, NG])
        goh = sb("goh", [P, T, NG])
        prod = sb("prod", [P, T, NG, EPG])
        se = [sb(f"se{i}", [P, T, EPG]) for i in range(2)]
        emx = [sb(f"emx{i}", [P, T, 1]) for i in range(2)]
        eeq = sb("eeq", [P, T, EPG])
        ecm = sb("ecm", [P, T, 1])
        eoh = [sb(f"eoh{i}", [P, T, EPG]) for i in range(2)]
        ed = sb("ed", [P, T, 1])
        eden = sb("eden", [P, T, 1])
        wk = [sb(f"wk{i}", [P, T, 1]) for i in range(2)]
        msk = [sb(f"msk{i}", [P, T, E]) for i in range(2)]
        mask = sb("mask", [P, T, E])
        cnt = sb("cnt", [P, E])
        endc = sb("endc", [P, E])
        offc = sb("offc", [P, E])
        posn = sb("posn", [P, T, E])
        slot_of = [sb(f"slot_of{i}", [P, T, 1]) for i in range(2)]
        off_i = sb("off_i", [1, E], I32)
        NC_ = SEQ // CAP - 1
        ov_ind = sb("ov_ind", [1, NC_, E])
        ov_n = sb("ov_n", [1, E])
        ov_end = sb("ov_end", [1, E])
        ov_rank = sb("ov_rank", [1, NC_, E])
        ov_start = sb("ov_start", [1, NC_, E])
        ov_tmp = sb("ov_tmp", [1, NC_, E])
        ov_last = sb("ov_last", [1, E])
        ov_dump = sb("ov_dump", [1, NC_, E])
        ov_f = sb("ov_f", [1, 2 * MAXOVF + 1])
        ov_i = sb("ov_i", [1, 2 * MAXOVF + 1], I32)

        bank = [ctx.enter_context(nc.psum_tensor(f"bank{i}", [P, 512], F32)) for i in range(8)]

        def gate_w(s):
            return ring[:, s, 0:2048].rearrange("p (k f) -> p k f", k=KC)

        def up_w(s):
            return ring[:, s, 2048:4096].rearrange("p (k f) -> p k f", k=KC)

        def down_w(s):
            return ring[:, s, 4096:6144].rearrange("p (j d) -> p j d", j=2)

        def cols_w(s, n):
            return ring[:, s, 0:KC * n].rearrange("p (k n) -> p k n", k=KC)

        gate_d = exp_w_gate.rearrange("l e (p k) f -> l e p (k f)", k=KC)
        up_d = exp_w_up.rearrange("l e (p k) f -> l e p (k f)", k=KC)
        down_d = exp_w_down.rearrange("l e (j p) d -> l e p j d", p=P)
        ada_d = ada_w.rearrange("l (p k) n -> l p k n", k=KC)
        qkv_d = w_qkv.rearrange("l (p k) n -> l p k n", k=KC)
        wo_d = w_o.rearrange("l (m p) n -> l p m n", p=P)
        poolw_d = pool_w.rearrange("l g (c p) d -> l p (g c) d", p=P)
        x_d = x.rearrange("b (t p) d -> (b p) t d", p=P)
        out_d = out.rearrange("b (t p) d -> (b p) t d", p=P)

        def full_at(n):
            return 48 * (n // R + 1)

        def pieces(j):
            lo, hi = j * AC, (j + 1) * AC
            cut = -(-(lo + 1) // 512) * 512
            return [(lo, cut), (cut, hi)]

        block = ctx.enter_context(nc.Block())

        @block.sync
        def _(sp):
            def split3(n, dst, src):
                if n >= R:
                    sp.wait_ge(S("ring_free", n % R), n // R)
                for a, b in ((0, 3), (3, 6), (6, 8)):
                    sp.dma_start(dst[:, a:b, :], src[:, a:b, :]).then_inc(S("ring_full", n % R), 16)

            def ada(a):
                L, j = divmod(a, 8)
                n = IT_ADA[a]
                split3(n, cols_w(n % R, AC), ada_d[L, :, :, j * AC:(j + 1) * AC])

            def expert(L, e, s, freed):
                if freed is not None:
                    sp.wait_ge(S("ring_free", s), freed)
                gsrc, usrc, dsrc = gate_d[L], up_d[L], down_d[L]
                sp.dma_start(ring[:, s, 0:2048], gsrc[bass.ds(e, 1), :, :].rearrange("a p n -> (a p) n"))\
                    .then_inc(S("ring_full", s), 16)
                sp.dma_start(ring[:, s, 2048:4096], usrc[bass.ds(e, 1), :, :].rearrange("a p n -> (a p) n"))\
                    .then_inc(S("ring_full", s), 16)
                sp.dma_start(down_w(s), dsrc[bass.ds(e, 1), :, :, :].rearrange("a p j d -> (a p) j d"))\
                    .then_inc(S("ring_full", s), 16)

            def experts(L, e0, e1):
                n0 = IT_EXP[L](e0)
                with sp.Fori(0, (e1 - e0) // R) as i:
                    for u in range(R):
                        n = n0 + u
                        expert(L, e0 + i * R + u, n % R, n // R + i)

            for a in range(4):
                ada(a)
            split3(IT_POOL, cols_w(IT_POOL % R, SEQ), poolw_d[0])
            for a in range(4, 8):
                ada(a)
            experts(0, 0, HEAD_E)
            for a in range(8, 12):
                ada(a)
            for e in range(HEAD_E, E):
                n = IT_EXP[0](e)
                expert(0, e, n % R, n // R)
            for j, n in enumerate(IT_QKV):
                split3(n, cols_w(n % R, AC), qkv_d[0, :, :, j * AC:(j + 1) * AC])
            for a in range(12, 16):
                ada(a)
            for j, n in enumerate(IT_WO):
                split3(n, cols_w(n % R, 512), wo_d[0, :, :, j * 512:(j + 1) * 512])
            experts(1, 0, E)
            for t in range(T):
                sp.wait_ge(S("result_ready"), t + 1)
                sp.dma_start(out_d[:, t, :], h[:, t, :]).then_inc(S("stored"), 16)
            sp.wait_ge(S("stored"), 16 * T)

        @block.gpsimd
        def _(pool):
            nc.gpsimd.memset(ones[:, :], 1.0).then_inc(S("ones_ready"), 1)
            pool.wait_ge(S("stage_loaded"), 32)
            nc.gpsimd.tensor_copy(rw[:, :, :, 0:NG], stage_g).then_inc(S("rw_ready"), 1)
            nc.gpsimd.tensor_copy(rw[:, :, :, NG:NG + E], stage_e).then_inc(S("rw_ready"), 1)

        @block.tensor
        def _(pe):
            def mm(o_, l_, r_, start, stop):
                return nc.tensor.matmul(o_, l_, r_, start=start, stop=stop)

            def row_bcast(o_, row, a, b, start=True):
                return mm(o_, ident[0:NROWS, row:row + 1].broadcast_to([NROWS, P]), rows[:, a:b], start, True)

            def bcast(a):
                L, j = divmod(a, 8)
                if a == 0:
                    pe.wait_ge(S("ones_ready"), 1)
                    pe.wait_ge(S("misc_loaded"), 16)
                    pe.wait_ge(S("rows_loaded"), 16 * 6)
                if a >= 1:
                    pe.wait_ge(S("mod_written"), 2 * a)
                pe.wait_ge(S("acc_ready"), 2 * (a + 1))
                c0 = j * AC
                for b, (lo, hi) in enumerate(pieces(j)):
                    row, col = divmod(lo, D)
                    dst = bank[4 + b][:, 0:hi - lo]
                    mm(dst, ones[:, :], acc[:, a % 2, lo - c0:hi - c0], True, False)
                    row_bcast(dst, ROW_B[L] + row, col, col + hi - lo, start=False)\
                        .then_inc(S("bcast_ready"), 1)

            def gain(row, b0, name):
                for b in range(2):
                    row_bcast(bank[b0 + b][:, :], row, b * 512, b * 512 + 512).then_inc(S(name), 1)

            def transposes(L, w):
                pe.wait_ge(S("h_ready", L, w), T)
                for b in range(4):
                    for kk in range(2):
                        for t in range(T):
                            last = nc.tensor.transpose(bank[b][:, kk * SEQ + t * P:kk * SEQ + (t + 1) * P],
                                                       h_str[:, t, 2 * b + kk, :], ident)
                    last.then_inc(S("hT_full", L, w), 1)

            def route(L):
                pe.wait_ge(S("hT_act", L, "ffn"), 2)
                pe.wait_ge(S("hT_dve", L, "ffn"), 2)
                if L == 0:
                    pe.wait_ge(S("rw_ready"), 2)
                for t in range(T):
                    for k in range(KC):
                        last = mm(bank[4][:, t * 36:t * 36 + 36], hT[:, k, t * P:(t + 1) * P], rw[:, L, k, :],
                                  k == 0, k == KC - 1)
                last.then_inc(S("logits", L), 1)
                pe.wait_ge(S("mask_ready", L), 1)
                for t in range(T):
                    mm(bank[5][:, 0:E], ones[:, :], mask[:, t, :], t == 0, t == T - 1)
                mm(bank[5][:, E:2 * E], tri, mask[:, 0, :], True, True)
                mm(bank[5][:, 2 * E:3 * E], ones[:, :], mask[:, 0, :], True, False)
                mm(bank[5][:, 2 * E:3 * E], tri, mask[:, 1, :], False, True).then_inc(S("counts", L), 1)

            def gather(L):
                pe.wait_ge(S("pick_ready", L), T)
                for k in range(KC):
                    if k >= 4:
                        pe.wait_ge(S("hS_ready", L), k - 3)
                    for t in range(T):
                        last = mm(bank[k % 4][:, :], h_str[:, t, k, :], pick[:, t, :], t == 0, t == T - 1)
                    last.then_inc(S("gathered", L), 1)
                pe.wait_ge(S("pickw_ready", L), T)
                for b in range(2):
                    for s in range(2):
                        for t in range(T):
                            last = nc.tensor.transpose(bank[6 + b][:, s * SEQ + t * P:s * SEQ + (t + 1) * P],
                                                       pickw[:, t, (2 * b + s) * P:(2 * b + s + 1) * P], ident)
                    last.then_inc(S("pwT_full", L), 1)
                pe.wait_ge(S("hS_ready", L), KC)

            def gate_up(dst, wg, wu, cols):
                for g, w in enumerate((wg, wu)):
                    for j in range(2):
                        c0 = (2 * g + j) * CAP
                        for k in range(KC):
                            last = mm(dst[:, c0:c0 + CAP], w[:, k, j * P:(j + 1) * P], hS[:, k, cols],
                                      k == 0, k == KC - 1)
                return last

            def down(dst, wd, hid):
                for m in range(KC):
                    for j in range(2):
                        last = mm(dst[:, m * CAP:(m + 1) * CAP], wd[:, j, m * P:(m + 1) * P],
                                  hid[:, j * CAP:(j + 1) * CAP], j == 0, j == 1)
                return last

            def expert(L, e, s, fill, b):
                off = pe.value_load(off_i[0:1, bass.ds(e, 1)], min_val=0, max_val=NSLOT)
                pe.wait_ge(S("ring_full", s), fill)
                pe.wait_ge(S("gu_free", L), e + 1)
                gate_up(bank[b], gate_w(s), up_w(s), bass.ds(off, CAP)).then_inc(S("gu_ready", L), 1)
                pe.wait_ge(S("he_ready", L), e + 1)
                pe.wait_ge(S("dn_free", L), e + 1)
                down(bank[2 + b], down_w(s), he[:, b, :]).then_inc(S("dn_ready", L), 1)

            def free_slot(L, s, e):
                pe.wait_ge(S("dn_ready", L), e + 1)
                pe.sem_inc(S("ring_free", s), 1)

            def experts(L, e0, e1):
                n0 = IT_EXP[L](e0)
                with pe.Fori(0, (e1 - e0) // R) as i:
                    for u in range(R):
                        n = n0 + u
                        e = i * R + (e0 + u)
                        expert(L, e, n % R, i * 48 + full_at(n), u % 2)
                        free_slot(L, n % R, e)

            def overflow(L):
                pe.wait_ge(S("ovf_ready", L), 1)
                n_ovf = pe.value_load(ov_i[0:1, 2 * MAXOVF:2 * MAXOVF + 1], min_val=0, max_val=MAXOVF)
                w = reg_h[:, :].rearrange("p (k f) -> p k f", k=KC)
                wd = reg_h[:, :].rearrange("p (j d) -> p j d", j=2)
                with pe.If(n_ovf > 0):
                    with pe.Fori(0, n_ovf) as i:
                        off = pe.value_load(ov_i[0:1, bass.ds(i + MAXOVF, 1)], min_val=0, max_val=NSLOT)
                        for g in range(2):
                            pe.wait_ge(S("ovf_w", L), i * 48 + 16 * (g + 1))
                            for j in range(2):
                                c0 = (2 * g + j) * CAP
                                for k in range(KC):
                                    last = mm(bank[0][:, c0:c0 + CAP], w[:, k, j * P:(j + 1) * P],
                                              hS[:, k, bass.ds(off, CAP)], k == 0, k == KC - 1)
                            last.then_inc(S("ovf_pe", L), 1)
                        pe.wait_ge(S("ovf_w", L), i * 48 + 48)
                        pe.wait_ge(S("ovf_he", L), i + 1)
                        down(bank[2], wd, he[:, 0, :]).then_inc(S("ovf_pe", L), 1)

            def combine(L):
                pe.wait_ge(S("yT_ready", L), 1)
                for f in range(2 * SB):
                    s, half = divmod(f, 2)
                    for mq in range(4):
                        last = nc.tensor.transpose(bank[f][:, mq * P:(mq + 1) * P],
                                                   yT[:, half * 4 + mq, s * P:(s + 1) * P], ident)
                    last.then_inc(S("yT_turned", L), 1)
                for half in range(2):
                    pe.wait_ge(S("yS_act" if half == 0 else "yS_dve", L), SB)
                    for t in range(T):
                        for s in range(SB):
                            last = mm(bank[half + 2 * t][:, :], pwT[:, s, t * P:(t + 1) * P],
                                      yS[:, s, half * 512:half * 512 + 512], s == 0, s == SB - 1)
                        last.then_inc(S("moe_out", L), 1)

            for a in range(4):
                bcast(a)
            gain(ROW_MIX, 6, "gain_mix_0")
            pe.wait_ge(S("h_ready", 0, "mix"), T)
            pe.wait_ge(S("band_loaded"), 16)
            for m in range(KC):
                for t in range(T):
                    last = mm(bank[m // 2][:, (m % 2) * SEQ:(m % 2 + 1) * SEQ], h[:, t, m * P:(m + 1) * P],
                              band_sb[:, t, m // 2, :], t == 0, t == T - 1)
                if m % 2:
                    last.then_inc(S("pT_full"), 1)
            pe.wait_ge(S("A_ready", 0, "mix"), 2)
            gain(ROW_PS, 6, "gain_ps")
            pe.wait_ge(S("pT_ready"), 4)
            pe.wait_ge(S("ring_full", IT_POOL % R), full_at(IT_POOL))
            pw = cols_w(IT_POOL % R, SEQ)
            for half in range(2):
                for t in range(T):
                    for gg in range(2):
                        for cc in range(2):
                            m = (2 * half + gg) * 2 + cc
                            last = mm(bank[half + 2 * t][:, gg * SEQ:(gg + 1) * SEQ], pT[:, m, t * P:(t + 1) * P],
                                      pw[:, m, :], cc == 0, cc == 1)
                    last.then_inc(S("mix_out", 0), 1)
            pe.wait_ge(S("mix_out", 0), 2 * T)
            pe.sem_inc(S("ring_free", IT_POOL % R), 1)
            for a in range(4, 8):
                bcast(a)
            pe.wait_ge(S("ps_used"), 2)
            gain(ROW_FFN, 6, "gain_ffn_0")
            transposes(0, "ffn")
            route(0)
            gather(0)
            experts(0, 0, HEAD_E)
            for a in range(8, 12):
                bcast(a)
            pe.wait_ge(S("pwT_ready", 0), 2)
            gain(ROW_MIX + 1, 6, "gain_mix_1")
            for e in range(HEAD_E, E):
                n = IT_EXP[0](e)
                expert(0, e, n % R, full_at(n), e % 2)
                free_slot(0, n % R, e)
            overflow(0)
            pe.wait_ge(S("A_ready", 1, "mix"), 2)
            combine(0)

            transposes(1, "mix")
            pe.wait_ge(S("hT_act", 1, "mix"), 2)
            pe.wait_ge(S("hT_dve", 1, "mix"), 2)
            u = 0
            for j, n in enumerate(IT_QKV):
                pe.wait_ge(S("ring_full", n % R), full_at(n))
                w = cols_w(n % R, AC)
                for col in range(j * AC, (j + 1) * AC, P):
                    m = col // P
                    if m >= 16 and m % 2:
                        continue
                    for t in range(1 if m < 16 else T):
                        if u >= 4:
                            pe.wait_ge(S("qkv_read"), u - 3)
                        for k in range(KC):
                            c0 = col - j * AC
                            if m < 16:
                                last = mm(bank[u % 4][:, 0:SEQ], w[:, k, c0:c0 + P], hT[:, k, :], k == 0, k == KC - 1)
                            else:
                                last = mm(bank[u % 4][:, 0:SEQ], hT[:, k, t * P:(t + 1) * P], w[:, k, c0:c0 + 256],
                                          k == 0, k == KC - 1)
                        last.then_inc(S("qkv_full"), 1)
                        u += 1
                pe.wait_ge(S("qkv_full"), u)
                pe.sem_inc(S("ring_free", n % R), 1)
                if j >= 1:
                    bcast(12 + j - 1)
            pe.wait_ge(S("qkv_read"), u)
            pe.wait_ge(S("mod_written"), 2 * 15)

            def scores(m, a):
                for t in range(T):
                    last = mm(bank[4 + a][:, t * P:t * P + (t + 1) * P], qT[a * DH:(a + 1) * DH, m, t * P:(t + 1) * P],
                              kT[a * DH:(a + 1) * DH, m, 0:(t + 1) * P], True, True)
                last.then_inc(S("s_full"), 1)

            def turn(hd, a):
                pe.wait_ge(S("p_ready"), 2 * hd + 2)
                for s in range(3):
                    last = nc.tensor.transpose(bank[6 + a][:, s * P:(s + 1) * P], pr[a][:, s * P:(s + 1) * P], ident)
                last.then_inc(S("pT_turned"), 1)

            def weigh(hd, m, a):
                pe.wait_ge(S("prT_ready"), hd + 1)
                cols = slice(a * DH, (a + 1) * DH)
                o_ = bank[0][a * DH:(a + 1) * DH, :]
                vm = v[:, :, bass.ds(m * P + a * DH, DH)]
                mm(o_[:, 0:SEQ], vm[:, 0, :], prT[a][:, 0:SEQ], True, False)
                mm(o_[:, P:SEQ], vm[:, 1, :], prT[a][:, SEQ:3 * P], False, True).then_inc(S("pv_done"), 1)

            def q_of(m):
                return m

            scores(0, 0)
            scores(0, 1)
            for m in range(NH // 2):
                for a in range(2):
                    hd = 2 * m + a
                    if hd >= 2:
                        pe.wait_ge(S("prT_ready"), hd - 1)
                    turn(hd, a)
                    if hd >= 1:
                        pm, pa = divmod(hd - 1, 2)
                        if pa == 0 and pm >= 1:
                            pe.wait_ge(S("o_read"), pm)
                        weigh(hd - 1, pm, pa)
                    if hd + 2 < NH:
                        pe.wait_ge(S("s_read"), hd + 1)
                        scores(m + 1, a)
            weigh(NH - 1, NH // 2 - 1, 1)
            pe.wait_ge(S("s_read"), NH)
            bcast(15)
            pe.wait_ge(S("prT_ready"), NH)
            gain(ROW_FFN + 1, 6, "gain_ffn_1")
            pe.wait_ge(S("o_read"), NH // 2)
            for j, n in enumerate(IT_WO):
                pe.wait_ge(S("ring_full", n % R), full_at(n))
                w = cols_w(n % R, 512)
                for t in range(T):
                    for m in range(KC):
                        last = mm(bank[j + 2 * t][:, :], oT[:, m, t * P:(t + 1) * P], w[:, m, :], m == 0, m == KC - 1)
                    last.then_inc(S("mix_out", 1), 1)
                pe.wait_ge(S("mix_out", 1), T * (j + 1))
                pe.sem_inc(S("ring_free", n % R), 1)
            transposes(1, "ffn")
            route(1)
            gather(1)
            experts(1, 0, E)
            overflow(1)
            pe.wait_ge(S("pwT_ready", 1), 2)
            combine(1)
            gain(ROW_FIN, 4, "gain_fin")

        @block.scalar
        def _(act):
            act.dma_start(ccol[:, :], c.rearrange("b (p k) -> (b p) k", k=KC)).then_inc(S("c_loaded"), 16)
            act.dma_start(cst[:, :], misc).then_inc(S("misc_loaded"), 16)
            for L in range(2):
                act.dma_start(rows[ROW_B[L]:ROW_B[L] + 6, :], ada_b[L].rearrange("(a d) -> a d", a=6))\
                    .then_inc(S("rows_loaded"), 16)
            act.dma_start(rows[ROW_MIX:ROW_MIX + 2, :], norm_mix_g).then_inc(S("rows_loaded"), 16)
            act.dma_start(rows[ROW_FFN:ROW_FFN + 2, :], norm_ffn_g).then_inc(S("rows_loaded"), 16)
            act.dma_start(rows[ROW_PS:ROW_PS + 1, :], pool_scale).then_inc(S("rows_loaded"), 16)
            act.dma_start(rows[ROW_FIN:ROW_FIN + 1, :], final_norm_g.rearrange("(a d) -> a d", a=1))\
                .then_inc(S("rows_loaded"), 16)
            act.dma_start(x_sb[:, :, :], x_d).then_inc(S("x_loaded"), 16)
            act.dma_start(band_sb, band.rearrange("p (t g q) -> p t g q", t=T, g=NG)).then_inc(S("band_loaded"), 16)
            act.dma_start(stage_g, router_group_w.rearrange("l (p k) n -> p l k n", k=KC)).then_inc(S("stage_loaded"), 16)
            act.dma_start(stage_e, router_expert_w.rearrange("l (p k) n -> p l k n", k=KC)).then_inc(S("stage_loaded"), 16)

            def copy(o_, i_):
                return nc.scalar.activation(o_, i_, ACT.Identity)

            def squares(L, w, waits, dump=reg_h):
                for t in range(T):
                    act.wait_ge(*waits(t))
                    nc.scalar.activation(dump[:, t * D:(t + 1) * D], x_sb[:, t, :], ACT.Square, accum_out=ss[:, t:t + 1])\
                        .then_inc(S("ss_ready", L, w), 1)

            def root(L, w):
                act.wait_ge(S("ms_ready", L, w), 1)
                nc.scalar.activation(rt[:, :], ms[:, :], ACT.Sqrt).then_inc(S("rt_ready", L, w), 1)

            def write_mod(a):
                for b, (lo, hi) in enumerate(pieces(a % 8)):
                    act.wait_ge(S("bcast_ready"), 2 * a + b + 1)
                    copy(mod[:, lo:hi], bank[4 + b][:, 0:hi - lo]).then_inc(S("mod_written"), 1)

            def evac_hT(L, w):
                for b in (0, 2):
                    act.wait_ge(S("hT_full", L, w), b + 1)
                    copy(hT[:, 2 * b:2 * b + 2, :], bank[b][:, :].rearrange("p (k q) -> p k q", k=2))\
                        .then_inc(S("hT_act", L, w), 1)

            def route(L):
                act.wait_ge(S("gd_ready", L), 1)
                nc.scalar.activation(gd[:, :, :], gd[:, :, :], ACT.Exp).then_inc(S("gexp", L), 1)
                act.wait_ge(S("ed_ready", L), 1)
                nc.scalar.activation(ed[:, :, :], ed[:, :, :], ACT.Exp).then_inc(S("gexp", L), 1)

            def evac_gather(L):
                for k in range(KC):
                    act.wait_ge(S("gathered", L), k + 1)
                    last = copy(hS[:, k, 0:NSLOT], bank[k % 4][:, :])
                    last.then_inc(S("hS_ready", L), 1)
                for b in range(2):
                    act.wait_ge(S("pwT_full", L), b + 1)
                    copy(pwT[:, 2 * b:2 * b + 2, :], bank[6 + b][:, :].rearrange("p (s q) -> p s q", s=2))\
                        .then_inc(S("pwT_ready", L), 1)
                act.wait_ge(S("hS_ready", L), KC)
                act.sem_inc(S("gu_free", L), 2)
                act.sem_inc(S("dn_free", L), 2)

            def expert(L, e, b):
                off = act.value_load(off_i[0:1, bass.ds(e, 1)], min_val=0, max_val=NSLOT)
                act.wait_ge(S("gu_ready", L), e + 1)
                nc.scalar.activation(sil[:, b, :], bank[b][:, 0:2 * CAP], ACT.Silu).then_inc(S("sil_ready", L), 1)
                act.wait_ge(S("dn_ready", L), e + 1)
                copy(yT[:, :, bass.ds(off, CAP)], bank[2 + b][:, :].rearrange("p (m s) -> p m s", m=KC))\
                    .then_inc(S("dn_free", L), 1)

            def experts(L, e0, e1):
                with act.Fori(0, (e1 - e0) // R) as i:
                    for u in range(R):
                        expert(L, i * R + (e0 + u), u % 2)

            def overflow(L):
                n_ovf = act.value_load(ov_i[0:1, 2 * MAXOVF:2 * MAXOVF + 1], min_val=0, max_val=MAXOVF)
                with act.If(n_ovf > 0):
                    with act.Fori(0, n_ovf) as i:
                        e = act.value_load(ov_i[0:1, bass.ds(i, 1)], min_val=0, max_val=E - 1)
                        off = act.value_load(ov_i[0:1, bass.ds(i + MAXOVF, 1)], min_val=0, max_val=NSLOT)
                        act.wait_ge(S("ovf_pe", L), i * 3)
                        act.dma_start(reg_h[:, :], gate_d[L][bass.ds(e, 1), :, :].rearrange("a p n -> (a p) n"))\
                            .then_inc(S("ovf_w", L), 16)
                        act.wait_ge(S("ovf_pe", L), i * 3 + 1)
                        act.dma_start(reg_h[:, :], up_d[L][bass.ds(e, 1), :, :].rearrange("a p n -> (a p) n"))\
                            .then_inc(S("ovf_w", L), 16)
                        act.wait_ge(S("ovf_pe", L), i * 3 + 2)
                        act.dma_start(reg_h[:, :].rearrange("p (j d) -> p j d", j=2),
                                      down_d[L][bass.ds(e, 1), :, :, :].rearrange("a p j d -> (a p) j d"))\
                            .then_inc(S("ovf_w", L), 16)
                        nc.scalar.activation(sil[:, 0, :], bank[0][:, 0:2 * CAP], ACT.Silu).then_inc(S("ovf_sil", L), 1)
                        act.wait_ge(S("ovf_pe", L), i * 3 + 3)
                        copy(yT[:, :, bass.ds(off, CAP)], bank[2][:, :].rearrange("p (m s) -> p m s", m=KC))\
                            .then_inc(S("ovf_y", L), 1)
                        act.wait_ge(S("ovf_y", L), i + 1)
                act.wait_ge(S("dn_free", L), E + 2)
                act.sem_inc(S("yT_ready", L), 1)

            def evac_yT(L):
                for f in range(0, 2 * SB, 2):
                    act.wait_ge(S("yT_turned", L), f + 1)
                    copy(yS[:, f // 2, 0:512], bank[f][:, :]).then_inc(S("yS_act", L), 1)

            act.wait_ge(S("c_loaded"), 16)
            nc.scalar.activation(cact[:, :], ccol[:, :], ACT.Silu).then_inc(S("cact_ready"), 1)
            squares(0, "mix", lambda t: (S("x_loaded"), 16))
            for a in range(4):
                write_mod(a)
            root(0, "mix")
            for b in range(4):
                act.wait_ge(S("pT_full"), b + 1)
                copy(pT[:, 2 * b:2 * b + 2, :], bank[b][:, :].rearrange("p (m q) -> p m q", m=2))\
                    .then_inc(S("pT_ready"), 1)
            for a in range(4, 8):
                write_mod(a)
            squares(0, "ffn", lambda t: (S("x_mixed", 0), 2 + t + 1))
            root(0, "ffn")
            evac_hT(0, "ffn")
            route(0)
            evac_gather(0)
            experts(0, 0, HEAD_E)
            for a in range(8, 12):
                write_mod(a)
            for e in range(HEAD_E, E):
                expert(0, e, e % 2)
            overflow(0)
            evac_yT(0)
            squares(1, "mix", lambda t: (S("x_moe", 0), 2 + t + 1))
            root(1, "mix")
            evac_hT(1, "mix")
            u = 0
            for j in range(4):
                for m in range(6 * j, 6 * j + 6):
                    if m >= 16 and m % 2:
                        continue
                    for t in range(1 if m < 16 else T):
                        act.wait_ge(S("qkv_full"), u + 1)
                        src = bank[u % 4][:, 0:SEQ]
                        if m < 8:
                            last = nc.scalar.activation(qT[:, m, :], src, ACT.Identity, scale=DH ** -0.5)
                        elif m < 16:
                            last = copy(kT[:, m - 8, :], src)
                        else:
                            last = copy(v[:, t, (m - 16) * P:(m - 14) * P], src)
                        last.then_inc(S("qkv_read"), 1)
                        u += 1
                if j >= 1:
                    write_mod(12 + j - 1)

            def exps(hd, a):
                act.wait_ge(S("mx_ready"), 2 * hd + 2)
                if hd >= 2:
                    act.wait_ge(S("pT_turned"), hd - 1)
                for t in range(T):
                    cols = slice(t * P, t * P + (t + 1) * P)
                    nc.scalar.activation(pr[a][:, cols], sc[a][:, cols], ACT.Exp, bias=nmx[:, a, t:t + 1],
                                         accum_out=psm[:, a, t:t + 1]).then_inc(S("exp_done"), 1)

            def evac_prT(hd, a):
                act.wait_ge(S("pT_turned"), hd + 1)
                if hd >= 2:
                    act.wait_ge(S("pv_done"), hd - 1)
                copy(prT[a], bank[6 + a][:, 0:3 * P]).then_inc(S("prT_ready"), 1)

            for hd in range(NH):
                exps(hd, hd % 2)
                if hd:
                    evac_prT(hd - 1, (hd - 1) % 2)
            evac_prT(NH - 1, 1)
            write_mod(15)
            squares(1, "ffn", lambda t: (S("x_mixed", 1), 2 + t + 1), dump=reg_b)
            root(1, "ffn")
            evac_hT(1, "ffn")
            route(1)
            evac_gather(1)
            experts(1, 0, E)
            overflow(1)
            evac_yT(1)
            squares(2, "fin", lambda t: (S("x_moe", 1), 2 + t + 1))
            root(2, "fin")

        @block.vector
        def _(dve):
            steps = [0]

            def then(ins):
                steps[0] += 1
                ins.then_inc(S("dve_step"), 1)
                dve.wait_ge(S("dve_step"), steps[0])

            def tt(o_, a_, b_, op):
                return nc.vector.tensor_tensor(o_, a_, b_, op)

            def stt(o_, a_, s_, b_, op0, op1):
                return nc.vector.scalar_tensor_tensor(o_, a_, s_, b_, op0, op1)

            def ada(a):
                n = IT_ADA[a]
                w = cols_w(n % R, AC)
                dve.wait_ge(S("ring_full", n % R), full_at(n))
                if a == 0:
                    dve.wait_ge(S("cact_ready"), 1)
                if a >= 2:
                    dve.wait_ge(S("bcast_ready"), 2 * (a - 1))
                for k in range(KC):
                    for hf in range(2):
                        cols = slice(hf * AC // 2, (hf + 1) * AC // 2)
                        dst = acc[:, a % 2, cols]
                        if k == 0:
                            ins = nc.vector.tensor_scalar(dst, w[:, k, cols], cact[:, k:k + 1], None, ALU.mult)
                        else:
                            dve.wait_ge(S("acc_step"), 2 * (KC - 1) * a + 2 * (k - 1) + hf + 1)
                            ins = stt(dst, w[:, k, cols], cact[:, k:k + 1], dst, ALU.mult, ALU.add)
                        if k < KC - 1:
                            ins.then_inc(S("acc_step"), 1)
                        else:
                            ins.then_inc(S("acc_ready"), 1)
                dve.wait_ge(S("acc_ready"), 2 * (a + 1))
                dve.sem_inc(S("ring_free", n % R), 1)

            def scale_vec(L, w, j, name):
                dve.wait_ge(S("mod_written"), 2 * (8 * L + 4 + (4 if w == "ffn" else 0)))
                for b in range(2):
                    dve.wait_ge(S(name), b + 1)
                    cols = slice(j * D + b * 512, j * D + b * 512 + 512)
                    stt(mod[:, cols], mod[:, cols], 1.0, bank[6 + b][:, :], ALU.add, ALU.mult)\
                        .then_inc(S("A_ready", L, w), 1)
                dve.wait_ge(S("A_ready", L, w), 2)

            def rstd(L, w):
                dve.wait_ge(S("ss_ready", L, w), T)
                nc.vector.tensor_scalar(ms[:, :], ss[:, :], 1.0 / D, EPS, ALU.mult, ALU.add)\
                    .then_inc(S("ms_ready", L, w), 1)
                dve.wait_ge(S("rt_ready", L, w), 1)
                then(nc.vector.reciprocal(rs[:, :], rt[:, :]))

            def norm(L, w, ja, jb):
                for t in range(T):
                    stt(h[:, t, :], x_sb[:, t, :], rs[:, t:t + 1], mod[:, ja * D:(ja + 1) * D], ALU.mult, ALU.mult)\
                        .then_inc(S("h_scaled", L, w), 1)
                for t in range(T):
                    dve.wait_ge(S("h_scaled", L, w), t + 1)
                    tt(h[:, t, :], h[:, t, :], mod[:, jb * D:(jb + 1) * D], ALU.add).then_inc(S("h_ready", L, w), 1)

            def add_to_x(ready, done, jg, tmp):
                for half in range(2):
                    cols = slice(half * 512, half * 512 + 512)
                    for t in range(T):
                        dve.wait_ge(ready, half * T + t + 1)
                        then(tt(tmp, bank[half + 2 * t][:, :], mod[:, jg * D + half * 512:jg * D + half * 512 + 512], ALU.mult))
                        tt(x_sb[:, t, cols], x_sb[:, t, cols], tmp, ALU.add).then_inc(done, 1)
                        dve.wait_ge(done, half * T + t + 1)

            def evac_hT(L, w):
                for b in (1, 3):
                    dve.wait_ge(S("hT_full", L, w), b + 1)
                    nc.vector.tensor_copy(hT[:, 2 * b:2 * b + 2, :], bank[b][:, :].rearrange("p (k q) -> p k q", k=2))\
                        .then_inc(S("hT_dve", L, w), 1)

            def wide(ap, n):
                return ap.broadcast_to([P, T, n])

            def first_max(val, mx, n, oh, eq, cm):
                then(nc.vector.tensor_reduce(mx, val, AX, ALU.max))
                then(tt(eq, val, wide(mx, n), ALU.is_equal))
                then(tt(eq, eq, first8[:, EPG - n:EPG].unsqueeze(1).broadcast_to([P, T, n]), ALU.mult))
                then(nc.vector.tensor_reduce(cm, eq, AX, ALU.max))
                then(tt(oh, eq, wide(cm, n), ALU.is_equal))

            def route(L):
                dve.wait_ge(S("logits", L), 1)
                then(nc.vector.tensor_copy(lg[:, :, :], bank[4][:, 0:T * 36].rearrange("p (t n) -> p t n", t=T)))
                first_max(lg[:, :, 0:NG], gm[:, :, :], NG, goh[:, :, :], geq[:, :, :], ecm[:, :, :])
                tt(gd[:, :, :], lg[:, :, 0:NG], wide(gm[:, :, :], NG), ALU.subtract).then_inc(S("gd_ready", L), 1)
                el = lg[:, :, NG:NG + E].rearrange("p t (g j) -> p t g j", g=NG)
                for t in range(T):
                    last = tt(prod[:, t, :, :], el[:, t, :, :],
                              goh[:, t, :].unsqueeze(2).broadcast_to([P, NG, EPG]), ALU.mult)
                then(last)
                then(nc.vector.tensor_reduce(se[0][:, :, :], prod[:, :, :, :].rearrange("p t g j -> p t j g"), AX, ALU.add))
                first_max(se[0][:, :, :], emx[0][:, :, :], EPG, eoh[0][:, :, :], eeq[:, :, :], ecm[:, :, :])
                then(stt(se[1][:, :, :], eoh[0][:, :, :], -BIG, se[0][:, :, :], ALU.mult, ALU.add))
                first_max(se[1][:, :, :], emx[1][:, :, :], EPG, eoh[1][:, :, :], eeq[:, :, :], ecm[:, :, :])
                tt(ed[:, :, :], emx[1][:, :, :], emx[0][:, :, :], ALU.subtract).then_inc(S("ed_ready", L), 1)
                for i in range(2):
                    for t in range(T):
                        last = tt(msk[i][:, t, :].rearrange("p (g j) -> p g j", g=NG),
                                  goh[:, t, :].unsqueeze(2).broadcast_to([P, NG, EPG]),
                                  eoh[i][:, t, :].unsqueeze(1).broadcast_to([P, NG, EPG]), ALU.mult)
                then(last)
                tt(mask[:, :, :], msk[0][:, :, :], msk[1][:, :, :], ALU.add).then_inc(S("mask_ready", L), 1)
                dve.wait_ge(S("gexp", L), 2)
                then(nc.vector.tensor_reduce(gsum[:, :, :], gd[:, :, :], AX, ALU.add))
                then(nc.vector.tensor_scalar(eden[:, :, :], ed[:, :, :], 1.0, None, ALU.add))
                then(tt(eden[:, :, :], eden[:, :, :], gsum[:, :, :], ALU.mult))
                then(nc.vector.reciprocal(wk[0][:, :, :], eden[:, :, :]))
                then(tt(wk[1][:, :, :], wk[0][:, :, :], ed[:, :, :], ALU.mult))
                dve.wait_ge(S("counts", L), 1)
                then(nc.vector.tensor_copy(cnt[:, :], bank[5][:, 0:E]))
                then(nc.vector.tensor_tensor_scan(endc[:, :], cnt[:, :], cnt[:, :], 0.0, ALU.add, ALU.bypass)
                     if False else nc.vector.tensor_tensor_scan(endc[:, :], ones[:, 0:E], cnt[:, :], 0.0, ALU.mult, ALU.add))
                then(tt(offc[:, :], endc[:, :], cnt[:, :], ALU.subtract))
                nc.vector.tensor_copy(off_i[:, :], offc[0:1, :]).then_inc(S("off_ready", L), 1)
                then(tt(posn[:, :, :], bank[5][:, E:3 * E].rearrange("p (t n) -> p t n", t=T),
                        offc[:, :].unsqueeze(1).broadcast_to([P, T, E]), ALU.add))
                for i in range(2):
                    then(tt(msk[i][:, :, :], msk[i][:, :, :], posn[:, :, :], ALU.mult))
                    then(nc.vector.tensor_reduce(slot_of[i][:, :, :], msk[i][:, :, :], AX, ALU.add))
                for t in range(T):
                    then(nc.vector.tensor_scalar(pick[:, t, :], iota, slot_of[0][:, t, :], None, ALU.is_equal))
                    stt(pick[:, t, :], iota, slot_of[1][:, t, :], pick[:, t, :], ALU.is_equal, ALU.add)\
                        .then_inc(S("pick_ready", L), 1)
                if L == 0:
                    dve.wait_ge(S("rw_ready"), 2)
                for t in range(T):
                    tmp = reg_c[:, 1024:1024 + NSLOT]
                    then(nc.vector.tensor_scalar(pickw[:, t, :], iota, slot_of[0][:, t, :], wk[0][:, t, :],
                                                 ALU.is_equal, ALU.mult))
                    then(nc.vector.tensor_scalar(tmp, iota, slot_of[1][:, t, :], wk[1][:, t, :],
                                                 ALU.is_equal, ALU.mult))
                    tt(pickw[:, t, :], pickw[:, t, :], tmp, ALU.add).then_inc(S("pickw_ready", L), 1)
                    dve.wait_ge(S("pickw_ready", L), t + 1)
                nc.vector.memset(hS[:, :, NSLOT:PAD], 0.0).then_inc(S("hS_pad", L), 1)
                overflow_list()
                ins = nc.vector.tensor_copy(ov_i[:, :], ov_f[:, :])
                ins.then_inc(S("ovf_ready", L), 1)

            def overflow_list():
                n1, end1, off1 = cnt[0:1, :], endc[0:1, :], offc[0:1, :]
                for q in range(NC_):
                    then(nc.vector.tensor_scalar(ov_ind[:, q, :], n1, float(CAP * (q + 1)), None, ALU.is_gt))
                then(nc.vector.tensor_reduce(ov_n[:, :], ov_ind[:, :, :].rearrange("p q e -> p e q"), AX, ALU.add))
                then(nc.vector.tensor_tensor_scan(ov_end[:, :], ones[0:1, 0:E], ov_n[:, :], 0.0, ALU.mult, ALU.add))
                then(tt(ov_n[:, :], ov_end[:, :], ov_n[:, :], ALU.subtract))
                then(nc.vector.tensor_scalar(ov_last[:, :], end1, -float(CAP), None, ALU.add))
                for q in range(NC_):
                    then(nc.vector.tensor_scalar(ov_rank[:, q, :], ov_n[:, :], float(q), None, ALU.add))
                    then(stt(ov_start[:, q, :], off1, float(CAP * (q + 1)), ov_last[:, :], ALU.add, ALU.min))
                for i in range(MAXOVF):
                    then(stt(ov_tmp[:, :, :], ov_rank[:, :, :], float(i), ov_ind[:, :, :], ALU.is_equal, ALU.mult))
                    then(nc.vector.tensor_tensor_reduce(
                        ov_dump[:, :, :], ov_tmp[:, :, :], iota[0:1, 0:E].unsqueeze(1).broadcast_to([1, NC_, E]),
                        1.0, 0.0, ALU.mult, ALU.add, ov_f[:, i:i + 1]))
                    then(nc.vector.tensor_tensor_reduce(
                        ov_dump[:, :, :], ov_tmp[:, :, :], ov_start[:, :, :],
                        1.0, 0.0, ALU.mult, ALU.add, ov_f[:, MAXOVF + i:MAXOVF + i + 1]))
                then(nc.vector.tensor_copy(ov_f[:, 2 * MAXOVF:2 * MAXOVF + 1], ov_end[:, E - 1:E]))

            def expert(L, e, b):
                dve.wait_ge(S("sil_ready", L), e + 1)
                dve.wait_ge(S("gu_ready", L), e + 1)
                tt(he[:, b, :], sil[:, b, :], bank[b][:, 2 * CAP:4 * CAP], ALU.mult).then_inc(S("he_ready", L), 1)
                dve.wait_ge(S("he_ready", L), e + 1)
                dve.sem_inc(S("gu_free", L), 1)

            def experts(L, e0, e1):
                with dve.Fori(0, (e1 - e0) // R) as i:
                    for u in range(R):
                        expert(L, i * R + (e0 + u), u % 2)

            def overflow(L):
                n_ovf = dve.value_load(ov_i[0:1, 2 * MAXOVF:2 * MAXOVF + 1], min_val=0, max_val=MAXOVF)
                with dve.If(n_ovf > 0):
                    with dve.Fori(0, n_ovf) as i:
                        dve.wait_ge(S("ovf_sil", L), i + 1)
                        tt(he[:, 0, :], sil[:, 0, :], bank[0][:, 2 * CAP:4 * CAP], ALU.mult).then_inc(S("ovf_he", L), 1)

            def evac_yT(L):
                for f in range(1, 2 * SB, 2):
                    dve.wait_ge(S("yT_turned", L), f + 1)
                    nc.vector.tensor_copy(yS[:, f // 2, 512:D], bank[f][:, :]).then_inc(S("yS_dve", L), 1)

            for a in range(4):
                ada(a)
            scale_vec(0, "mix", 1, "gain_mix_0")
            rstd(0, "mix")
            norm(0, "mix", 1, 0)
            ada(4)
            for b in range(2):
                dve.wait_ge(S("gain_ps"), b + 1)
                cols = slice(2 * D + b * 512, 2 * D + b * 512 + 512)
                tt(mod[:, cols], mod[:, cols], bank[6 + b][:, :], ALU.mult).then_inc(S("ps_used"), 1)
            dve.wait_ge(S("ps_used"), 2)
            ada(5)
            add_to_x(S("mix_out", 0), S("x_mixed", 0), 2, reg_b[:, 0:512])
            ada(6)
            ada(7)
            scale_vec(0, "ffn", 4, "gain_ffn_0")
            rstd(0, "ffn")
            norm(0, "ffn", 4, 3)
            evac_hT(0, "ffn")
            route(0)
            experts(0, 0, HEAD_E)
            for a in range(8, 12):
                ada(a)
            scale_vec(1, "mix", 1, "gain_mix_1")
            for e in range(HEAD_E, E):
                expert(0, e, e % 2)
            overflow(0)
            evac_yT(0)
            add_to_x(S("moe_out", 0), S("x_moe", 0), 5, reg_c[:, 1024:1536])

            rstd(1, "mix")
            norm(1, "mix", 1, 0)
            evac_hT(1, "mix")
            for a in range(12, 16):
                ada(a)

            def front(hd, a):
                dve.wait_ge(S("s_full"), hd + 1)
                if hd >= 2:
                    dve.wait_ge(S("exp_done"), 2 * hd - 2)
                stt(sc[a], alibi, slopes[:, hd:hd + 1], bank[4 + a][:, 0:3 * P], ALU.mult, ALU.add)\
                    .then_inc(S("s_read"), 1)
                dve.wait_ge(S("s_read"), hd + 1)
                for t in range(T):
                    nc.vector.tensor_reduce(nmx[:, a, t:t + 1], sc[a][:, t * P:t * P + (t + 1) * P], AX, ALU.max,
                                            negate=True).then_inc(S("mx_ready"), 1)

            def back(hd, a):
                dve.wait_ge(S("exp_done"), 2 * hd + 2)
                then(nc.vector.reciprocal(prc[:, a, :], psm[:, a, :]))
                for t in range(T):
                    cols = slice(t * P, t * P + (t + 1) * P)
                    nc.vector.tensor_scalar(pr[a][:, cols], pr[a][:, cols], prc[:, a, t:t + 1], None, ALU.mult)\
                        .then_inc(S("p_ready"), 1)

            def evac_o(m):
                dve.wait_ge(S("pv_done"), 2 * m + 2)
                nc.vector.tensor_copy(oT[:, m, :], bank[0][:, 0:SEQ]).then_inc(S("o_read"), 1)

            front(0, 0)
            for hd in range(NH):
                if hd + 1 < NH:
                    front(hd + 1, (hd + 1) % 2)
                back(hd, hd % 2)
                if hd >= 3 and hd % 2:
                    evac_o((hd - 3) // 2)
            evac_o(NH // 2 - 1)
            scale_vec(1, "ffn", 4, "gain_ffn_1")
            add_to_x(S("mix_out", 1), S("x_mixed", 1), 2, reg_a[:, 0:512])
            rstd(1, "ffn")
            norm(1, "ffn", 4, 3)
            evac_hT(1, "ffn")
            route(1)
            experts(1, 0, E)
            overflow(1)
            evac_yT(1)
            add_to_x(S("moe_out", 1), S("x_moe", 1), 5, reg_c[:, 1024:1536])
            rstd(2, "fin")
            for t in range(T):
                for b in range(2):
                    dve.wait_ge(S("gain_fin"), b + 1)
                    cols = slice(b * 512, b * 512 + 512)
                    last = stt(h[:, t, cols], x_sb[:, t, cols], rs[:, t:t + 1], bank[4 + b][:, :], ALU.mult, ALU.mult)
                last.then_inc(S("result_ready"), 1)


_INS = ["x", "c", "ada_w", "ada_b", "norm_mix_g", "norm_ffn_g", "pool_w", "pool_scale", "w_qkv", "w_o",
        "router_group_w", "router_expert_w", "exp_w_gate", "exp_w_up", "exp_w_down", "final_norm_g"]


def kernel(**inputs):
    import numpy as _np
    import concourse.bacc as _bacc
    from concourse import mybir as _mybir
    from concourse.bass_utils import run_bass_kernel_spmd as _run

    nc = _bacc.Bacc("TRN2", target_bir_lowering=False, num_devices=1)
    arrays, args = {}, {}
    for name, a in [(n, inputs[n]) for n in _INS] + list(constants().items()):
        a = _np.ascontiguousarray(a)
        arrays[f"in_{name}_dram"] = a
        args[name] = nc.dram_tensor(f"in_{name}_dram", a.shape, _mybir.dt.from_np(a.dtype), kind="ExternalInput").ap()
    out = nc.dram_tensor("out_0_dram", (1, SEQ, D), _mybir.dt.float32, kind="ExternalOutput").ap()
    program(nc, **args, out=out)
    r = _run(nc, [arrays], core_ids=[0])
    return r.results[0]["out_0_dram"]
```

```python
from contextlib import ExitStack

import numpy as np

import concourse.bass as bass
from concourse import mybir

P = 128
SEQ, D, F, E = 256, 1024, 256, 32
NG, EPG, TOPK = 4, 8, 2
NH, DH = 16, 64
T = SEQ // P
KC = D // P
NSLOT = SEQ * TOPK
SB = NSLOT // P
CAP = 64
PAD = NSLOT + CAP
MAXOVF = NSLOT // CAP - 1
R = 4
SLOT = 3 * D * F // P
AC = SLOT // KC
WINDOWS = (2, 4, 8, 16)
EPS = 1e-6
BIG = 3.0e38
MASKED = -1.0e30

ALU = mybir.AluOpType
ACT = mybir.ActivationFunctionType
F32 = mybir.dt.float32
I32 = mybir.dt.int32
AX = mybir.AxisListType.X

IT_ADA = [0, 1, 2, 3, 5, 6, 7, 8] + [37, 38, 39, 40, 49, 50, 51, 52]
IT_POOL = 4
HEAD_E = 28
IT_EXP = [lambda e: 9 + e if isinstance(e, int) and e < HEAD_E else 41 + e - HEAD_E, lambda e: 55 + e]

IT_QKV = [45, 46, 47, 48]
IT_WO = [53, 54]

ROW_B = [0, 6]
ROW_MIX, ROW_FFN, ROW_PS, ROW_FIN = 12, 14, 16, 17
NROWS = 18


def constants():
    ident = np.eye(P, dtype=np.float32)
    tri = np.triu(np.ones((P, P), np.float32), 1)
    iota = np.broadcast_to(np.arange(NSLOT, dtype=np.float32), (P, NSLOT)).copy()
    pos = np.arange(SEQ)
    band = np.zeros((SEQ, len(WINDOWS), SEQ), np.float32)
    for g, w in enumerate(WINDOWS):
        inside = (pos[:, None] <= pos[None, :]) & (pos[:, None] > pos[None, :] - w)
        band[:, g] = inside / np.minimum(pos + 1, w)[None, :] - np.eye(SEQ)
    band = np.ascontiguousarray(band.reshape(T, P, -1).transpose(1, 0, 2).reshape(P, -1).astype(np.float32))
    dist = pos[:, None] - pos[None, :]
    alibi = np.where(dist >= 0, -dist, MASKED).astype(np.float32)
    alibi = np.concatenate([alibi[:P, :P], alibi[P:, :]], 1)
    slopes = np.broadcast_to((2.0 ** (-8.0 * np.arange(1, NH + 1) / NH)).astype(np.float32), (P, NH)).copy()
    first8 = np.broadcast_to(np.arange(EPG, 0, -1, dtype=np.float32), (P, EPG)).copy()
    misc = np.concatenate([ident, tri, iota, alibi, slopes, first8], 1)
    return {"misc": np.ascontiguousarray(misc), "band": band}


def program(nc, x, c, ada_w, ada_b, norm_mix_g, norm_ffn_g, pool_w, pool_scale, w_qkv, w_o,
            router_group_w, router_expert_w, exp_w_gate, exp_w_up, exp_w_down, final_norm_g, misc, band, out):
    ctx = ExitStack()
    with ctx:
        def sb(name, shape, dt=F32):
            return ctx.enter_context(nc.sbuf_tensor(name, shape, dt))

        sems = {}

        def S(*name):
            key = "_".join(map(str, name))
            if key not in sems:
                sems[key] = ctx.enter_context(nc.semaphore(key))
            return sems[key]

        x_sb = sb("x_sb", [P, T, D])
        mod = sb("mod", [P, 6 * D])
        NM = 2 * P + NSLOT + 3 * P + NH + EPG
        cst = sb("cst", [P, NM])
        ident, tri = cst[:, 0:P], cst[:, P:2 * P]
        iota = cst[:, 2 * P:2 * P + NSLOT]
        o = 2 * P + NSLOT
        alibi, slopes, first8 = cst[:, o:o + 3 * P], cst[:, o + 3 * P:o + 3 * P + NH], cst[:, o + 3 * P + NH:NM]
        ones = sb("ones", [P, P])
        rows = sb("rows", [NROWS, D])
        ccol = sb("ccol", [P, KC])
        cact = sb("cact", [P, KC])
        acc = sb("acc", [P, 2, AC])
        ring = sb("ring", [P, R, SLOT])
        rw = sb("rw", [P, 2, KC, NG + E])
        reg_h = sb("reg_h", [P, T * D])
        reg_a = sb("reg_a", [P, KC * PAD])
        reg_b = sb("reg_b", [P, KC * PAD])
        reg_c = sb("reg_c", [P, 15 * P])

        h = reg_h[:, :].rearrange("p (t d) -> p t d", t=T)
        h_str = reg_h[:, :].rearrange("p (t q k) -> p t k q", t=T, k=KC)
        oT = reg_h[:, :].rearrange("p (m q) -> p m q", m=KC)
        hT = reg_b[:, 0:KC * SEQ].rearrange("p (k q) -> p k q", k=KC)
        band_sb = reg_a[:, 0:T * NG * SEQ].rearrange("p (t g q) -> p t g q", t=T, g=NG)
        pT = reg_a[:, 2048:2048 + KC * SEQ].rearrange("p (m q) -> p m q", m=KC)
        hS = reg_a[:, :].rearrange("p (k s) -> p k s", k=KC)
        yS = reg_a[:, 0:SB * D].rearrange("p (s d) -> p s d", s=SB)
        yT = reg_b[:, :].rearrange("p (m s) -> p m s", m=KC)
        pick = reg_b[:, 2048:2048 + T * NSLOT].rearrange("p (t s) -> p t s", t=T)
        pickw = reg_b[:, 3072:3072 + T * NSLOT].rearrange("p (t s) -> p t s", t=T)
        pwT = reg_c[:, 0:SB * SEQ].rearrange("p (s q) -> p s q", s=SB)
        stage_g = reg_c[:, 0:2 * KC * NG].rearrange("p (l k n) -> p l k n", l=2, k=KC)
        stage_e = reg_c[:, 64:64 + 2 * KC * E].rearrange("p (l k n) -> p l k n", l=2, k=KC)
        qT = reg_a[:, 0:2048].rearrange("p (m q) -> p m q", m=KC)
        kT = reg_a[:, 2048:4096].rearrange("p (m q) -> p m q", m=KC)
        v = reg_b[:, 2048:4096].rearrange("p (t d) -> p t d", t=T)
        sc = [reg_c[:, 3 * P * b:3 * P * (b + 1)] for b in range(2)]
        pr = [reg_c[:, 3 * P * (2 + b):3 * P * (3 + b)] for b in range(2)]
        prT = [reg_c[:, 12 * P:15 * P], reg_b[:, 4096:4096 + 3 * P]]

        ss = sb("ss", [P, T])
        ms = sb("ms", [P, T])
        rt = sb("rt", [P, T])
        rs = sb("rs", [P, T])
        nmx = sb("nmx", [P, 2, T])
        psm = sb("psm", [P, 2, T])
        prc = sb("prc", [P, 2, T])
        xe = sb("xe", [P, 2, KC, CAP])
        sil = reg_c[:, 1024:1280].rearrange("p (b f) -> p b f", b=2)
        he = reg_c[:, 1280:1536].rearrange("p (b f) -> p b f", b=2)
        heT = sb("heT", [P, 2, 2 * CAP])
        ye = sb("ye", [P, 2, D // 2])
        taken = [0]

        def scratch(shape):
            n = int(np.prod(shape[1:]))
            ap = ye[0:shape[0], :, :].rearrange("p b d -> p (b d)")[:, taken[0]:taken[0] + n]
            taken[0] += n
            assert taken[0] <= 2 * (D // 2)
            if len(shape) == 3:
                return ap.rearrange("p (a b) -> p a b", a=shape[1])
            return ap.rearrange("p (a b c) -> p a b c", a=shape[1], b=shape[2]) if len(shape) == 4 else ap

        lg = scratch([P, T, NG + E])
        gm = scratch([P, T, 1])
        gd = scratch([P, T, NG])
        gsum = scratch([P, T, 1])
        geq = scratch([P, T, NG])
        goh = scratch([P, T, NG])
        prod = scratch([P, T, NG, EPG])
        se = [scratch([P, T, EPG]) for i in range(2)]
        emx = [scratch([P, T, 1]) for i in range(2)]
        eeq = scratch([P, T, EPG])
        ecm = scratch([P, T, 1])
        eoh = [scratch([P, T, EPG]) for i in range(2)]
        ed = scratch([P, T, 1])
        eden = scratch([P, T, 1])
        wk = [scratch([P, T, 1]) for i in range(2)]
        msk = [scratch([P, T, E]) for i in range(2)]
        mask = scratch([P, T, E])
        cnt = scratch([P, E])
        endc = scratch([P, E])
        offc = scratch([P, E])
        posn = scratch([P, T, E])
        slot_of = [scratch([P, T, 1]) for i in range(2)]
        off_i = sb("off_i", [1, 2, E], I32)
        NC_ = SEQ // CAP - 1
        ov_ind = scratch([1, NC_, E])
        ov_n = scratch([1, E])
        ov_end = scratch([1, E])
        ov_rank = scratch([1, NC_, E])
        ov_start = scratch([1, NC_, E])
        ov_tmp = reg_c[0:1, 1536:1536 + NC_ * E].rearrange("p (q e) -> p q e", q=NC_)
        ov_last = scratch([1, E])
        ov_dump = reg_c[0:1, 1632:1632 + NC_ * E].rearrange("p (q e) -> p q e", q=NC_)
        ov_f = scratch([1, 2 * MAXOVF + 1])
        ov_i = sb("ov_i", [1, 2, 2 * MAXOVF + 1], I32)

        bank = [ctx.enter_context(nc.psum_tensor(f"bank{i}", [P, 512], F32)) for i in range(8)]

        def gate_w(s):
            return ring[:, s, 0:2048].rearrange("p (k f) -> p k f", k=KC)

        def up_w(s):
            return ring[:, s, 2048:4096].rearrange("p (k f) -> p k f", k=KC)

        def down_w(s):
            return ring[:, s, 4096:6144].rearrange("p (j d) -> p j d", j=2)

        def cols_w(s, n):
            return ring[:, s, 0:KC * n].rearrange("p (k n) -> p k n", k=KC)

        gate_d = exp_w_gate.rearrange("l e (p k) f -> l e p (k f)", k=KC)
        up_d = exp_w_up.rearrange("l e (p k) f -> l e p (k f)", k=KC)
        down_d = exp_w_down.rearrange("l e (j p) d -> l e p j d", p=P)
        ada_d = ada_w.rearrange("l (p k) n -> l p k n", k=KC)
        qkv_d = w_qkv.rearrange("l (p k) n -> l p k n", k=KC)
        wo_d = w_o.rearrange("l (m p) n -> l p m n", p=P)
        poolw_d = pool_w.rearrange("l g (c p) d -> l p (g c) d", p=P)
        x_d = x.rearrange("b (t p) d -> (b p) t d", p=P)
        out_d = out.rearrange("b (t p) d -> (b p) t d", p=P)

        def full_at(n):
            return 48 * (n // R + 1)

        def pieces(j):
            lo, hi = j * AC, (j + 1) * AC
            cut = -(-(lo + 1) // 512) * 512
            return [(lo, cut), (cut, hi)]

        def nth(L, w):
            return 2 * L + (w == "ffn")

        block = ctx.enter_context(nc.Block())

        @block.sync
        def _(sp):
            def split3(n, dst, src):
                if n >= R:
                    sp.wait_ge(S("ring_free", n % R), n // R)
                for a, b in ((0, 3), (3, 6), (6, 8)):
                    sp.dma_start(dst[:, a:b, :], src[:, a:b, :]).then_inc(S("ring_full", n % R), 16)

            def ada(a):
                L, j = divmod(a, 8)
                n = IT_ADA[a]
                split3(n, cols_w(n % R, AC), ada_d[L, :, :, j * AC:(j + 1) * AC])

            def expert(L, e, s, freed):
                if freed is not None:
                    sp.wait_ge(S("ring_free", s), freed)
                gsrc, usrc, dsrc = gate_d[L], up_d[L], down_d[L]
                sp.dma_start(ring[:, s, 0:2048], gsrc[bass.ds(e, 1), :, :].rearrange("a p n -> (a p) n"))\
                    .then_inc(S("ring_full", s), 16)
                sp.dma_start(ring[:, s, 2048:4096], usrc[bass.ds(e, 1), :, :].rearrange("a p n -> (a p) n"))\
                    .then_inc(S("ring_full", s), 16)
                sp.dma_start(down_w(s), dsrc[bass.ds(e, 1), :, :, :].rearrange("a p j d -> (a p) j d"))\
                    .then_inc(S("ring_full", s), 16)

            def experts(L, e0, e1):
                n0 = IT_EXP[L](e0)
                with sp.Fori(0, (e1 - e0) // R) as i:
                    for u in range(R):
                        n = n0 + u
                        expert(L, e0 + i * R + u, n % R, n // R + i)

            for a in range(4):
                ada(a)
            split3(IT_POOL, cols_w(IT_POOL % R, SEQ), poolw_d[0])
            for a in range(4, 8):
                ada(a)
            experts(0, 0, HEAD_E)
            for a in range(8, 12):
                ada(a)
            for e in range(HEAD_E, E):
                n = IT_EXP[0](e)
                expert(0, e, n % R, n // R)
            for j, n in enumerate(IT_QKV):
                split3(n, cols_w(n % R, AC), qkv_d[0, :, :, j * AC:(j + 1) * AC])
            for a in range(12, 16):
                ada(a)
            for j, n in enumerate(IT_WO):
                split3(n, cols_w(n % R, 512), wo_d[0, :, :, j * 512:(j + 1) * 512])
            experts(1, 0, E)
            for t in range(T):
                sp.wait_ge(S("result_ready"), t + 1)
                sp.dma_start(out_d[:, t, :], h[:, t, :]).then_inc(S("stored"), 16)
            sp.wait_ge(S("stored"), 16 * T)

        @block.gpsimd
        def _(pool):
            nc.gpsimd.memset(ones[:, :], 1.0).then_inc(S("ones_ready"), 1)
            pool.wait_ge(S("stage_loaded"), 32)
            nc.gpsimd.tensor_copy(rw[:, :, :, 0:NG], stage_g).then_inc(S("rw_ready"), 1)
            nc.gpsimd.tensor_copy(rw[:, :, :, NG:NG + E], stage_e).then_inc(S("rw_ready"), 1)

            def pick_tokens(L, e, b):
                off = pool.value_load(off_i[0:1, L, bass.ds(e, 1)], min_val=0, max_val=NSLOT)
                nc.gpsimd.tensor_copy(xe[:, b, :, :], hS[:, :, bass.ds(off, CAP)]).then_inc(S("xe_ready", L), 1)

            for L in range(2):
                pool.wait_ge(S("off_ready"), L + 1)
                pool.wait_ge(S("hS_ready"), L * KC + KC)
                pool.wait_ge(S("hS_pad"), L + 1)
                pick_tokens(L, 0, 0)
                pick_tokens(L, 1, 1)
                with pool.Fori(1, E // 2) as i:
                    for b in range(2):
                        pool.wait_ge(S("gu_ready", L), i * 2 + (b - 1))
                        pick_tokens(L, i * 2 + b, b)
                pool.wait_ge(S("ovf_ready"), L + 1)
                pool.wait_ge(S("gu_ready", L), E)
                n_ovf = pool.value_load(ov_i[0:1, L, 2 * MAXOVF:2 * MAXOVF + 1], min_val=0, max_val=MAXOVF)
                with pool.If(n_ovf > 0):
                    with pool.Fori(0, n_ovf) as i:
                        off = pool.value_load(ov_i[0:1, L, bass.ds(i + MAXOVF, 1)], min_val=0, max_val=NSLOT)
                        pool.wait_ge(S("ovf_pe", L), i * 3)
                        nc.gpsimd.tensor_copy(xe[:, 0, :, :], hS[:, :, bass.ds(off, CAP)]).then_inc(S("ovf_xe", L), 1)

        @block.tensor
        def _(pe):
            def mm(o_, l_, r_, start, stop):
                return nc.tensor.matmul(o_, l_, r_, start=start, stop=stop)

            def row_bcast(o_, row, a, b, start=True):
                return mm(o_, ident[0:NROWS, row:row + 1].broadcast_to([NROWS, P]), rows[:, a:b], start, True)

            def bcast(a):
                L, j = divmod(a, 8)
                if a == 0:
                    pe.wait_ge(S("ones_ready"), 1)
                    pe.wait_ge(S("misc_loaded"), 16)
                    pe.wait_ge(S("rows_loaded"), 16 * 6)
                if a >= 1:
                    pe.wait_ge(S("mod_written"), 2 * a)
                pe.wait_ge(S("acc_ready"), 2 * (a + 1))
                c0 = j * AC
                for b, (lo, hi) in enumerate(pieces(j)):
                    row, col = divmod(lo, D)
                    dst = bank[4 + b][:, 0:hi - lo]
                    mm(dst, ones[:, :], acc[:, a % 2, lo - c0:hi - c0], True, False)
                    row_bcast(dst, ROW_B[L] + row, col, col + hi - lo, start=False)\
                        .then_inc(S("bcast_ready"), 1)

            def gain(row, b0, name):
                for b in range(2):
                    row_bcast(bank[b0 + b][:, :], row, b * 512, b * 512 + 512).then_inc(S(name), 1)

            def transposes(L, w):
                pe.wait_ge(S("h_ready"), nth(L, w) * T + T)
                for b in range(4):
                    for kk in range(2):
                        for t in range(T):
                            last = nc.tensor.transpose(bank[b][:, kk * SEQ + t * P:kk * SEQ + (t + 1) * P],
                                                       h_str[:, t, 2 * b + kk, :], ident)
                    last.then_inc(S("hT_full"), 1)

            def route(L):
                pe.wait_ge(S("hT_act"), (nth(L, "ffn") - 1) * 2 + 2)
                pe.wait_ge(S("hT_dve"), (nth(L, "ffn") - 1) * 2 + 2)
                if L == 0:
                    pe.wait_ge(S("rw_ready"), 2)
                for t in range(T):
                    for k in range(KC):
                        last = mm(bank[4][:, t * 36:t * 36 + 36], hT[:, k, t * P:(t + 1) * P], rw[:, L, k, :],
                                  k == 0, k == KC - 1)
                last.then_inc(S("logits"), 1)
                pe.wait_ge(S("mask_ready"), L + 1)
                for t in range(T):
                    mm(bank[5][:, 0:E], ones[:, :], mask[:, t, :], t == 0, t == T - 1)
                mm(bank[5][:, E:2 * E], tri, mask[:, 0, :], True, True)
                mm(bank[5][:, 2 * E:3 * E], ones[:, :], mask[:, 0, :], True, False)
                mm(bank[5][:, 2 * E:3 * E], tri, mask[:, 1, :], False, True).then_inc(S("counts"), 1)

            def gather(L):
                pe.wait_ge(S("pick_ready"), L * T + T)
                for k in range(KC):
                    if k >= 4:
                        pe.wait_ge(S("hS_ready"), L * KC + k - 3)
                    for t in range(T):
                        last = mm(bank[k % 4][:, :], h_str[:, t, k, :], pick[:, t, :], t == 0, t == T - 1)
                    last.then_inc(S("gathered"), 1)
                pe.wait_ge(S("pickw_ready"), L * T + T)
                for b in range(2):
                    for s in range(2):
                        for t in range(T):
                            last = nc.tensor.transpose(bank[6 + b][:, s * SEQ + t * P:s * SEQ + (t + 1) * P],
                                                       pickw[:, t, (2 * b + s) * P:(2 * b + s + 1) * P], ident)
                    last.then_inc(S("pwT_full"), 1)

            def hidden(dst, w, b):
                for k in range(KC):
                    for j in range(2):
                        last = mm(dst[j * CAP:(j + 1) * CAP, :], xe[:, b, k, :], w(k, j), k == 0, k == KC - 1)
                return last

            def turn_he(dst, b):
                return nc.tensor.transpose(dst[:, 2 * P:3 * P], he[:, b, :], ident)

            def down(dst, wd, b):
                for j in range(2):
                    for half in range(2):
                        last = mm(dst[half * CAP:(half + 1) * CAP, :], heT[:, b, j * CAP:(j + 1) * CAP],
                                  wd[:, j, :].rearrange("p (c h q) -> p h c q", c=4, h=2)[:, half, :, :],
                                  j == 0, j == 1)
                return last

            def turn_ye(dst, b):
                for cq in range(4):
                    last = nc.tensor.transpose(dst[:, cq * P:(cq + 1) * P], ye[:, b, cq * P:(cq + 1) * P], ident)
                return last

            def expert(L, e, s, fill, b, first=False):
                gu = ring[:, s, 0:4096].rearrange("p (g k j f) -> p k j g f", g=2, k=KC, j=2)
                pe.wait_ge(S("xe_ready", L), e + 1)
                pe.wait_ge(S("ring_full", s), fill)
                pe.wait_ge(S("heT_ready", L), e + 1)
                hidden(bank[b][:, 0:F], lambda k, j: gu[:, k, j, :, :], b).then_inc(S("gu_ready", L), 1)
                if not first:
                    turn_last(L, e, 1 - b)
                pe.wait_ge(S("he_ready", L), e + 1)
                turn_he(bank[b], b).then_inc(S("he_turned", L), 1)
                pe.wait_ge(S("heT_ready", L), e + 3)
                pe.wait_ge(S("dn_free", L), e + 1)
                down(bank[2 + b], down_w(s), b).then_inc(S("dn_ready", L), 1)

            def turn_last(L, e, b):
                pe.wait_ge(S("ye_ready", L), e)
                turn_ye(bank[2 + b], b).then_inc(S("ye_turned", L), 1)

            def experts(L, e0, e1):
                n0 = IT_EXP[L](e0)
                with pe.Fori(0, (e1 - e0) // R) as i:
                    for u in range(R):
                        n = n0 + u
                        expert(L, i * R + (e0 + u), n % R, i * 48 + full_at(n), u % 2)

            def expert_at(L, e):
                n = IT_EXP[L](e)
                expert(L, e, n % R, full_at(n), e % 2, first=e == 0)

            def overflow(L):
                pe.wait_ge(S("ovf_ready"), L + 1)
                n_ovf = pe.value_load(ov_i[0:1, L, 2 * MAXOVF:2 * MAXOVF + 1], min_val=0, max_val=MAXOVF)
                w = reg_h[:, :].rearrange("p (k j f) -> p k j f", k=KC, j=2)
                wd = reg_h[:, :].rearrange("p (j d) -> p j d", j=2)
                with pe.If(n_ovf > 0):
                    with pe.Fori(0, n_ovf) as i:
                        pe.wait_ge(S("ovf_xe", L), i + 1)
                        for g in range(2):
                            pe.wait_ge(S("ovf_w", L), i * 48 + 16 * (g + 1))
                            hidden(bank[0][:, g * P:(g + 1) * P], lambda k, j: w[:, k, j, :], 0)\
                                .then_inc(S("ovf_pe", L), 1)
                        pe.wait_ge(S("ovf_he", L), i + 1)
                        turn_he(bank[0], 0).then_inc(S("ovf_he_turned", L), 1)
                        pe.wait_ge(S("ovf_w", L), i * 48 + 48)
                        pe.wait_ge(S("ovf_heT", L), i + 1)
                        down(bank[2], wd, 0).then_inc(S("ovf_pe", L), 1)
                        pe.wait_ge(S("ovf_ye", L), i + 1)
                        turn_ye(bank[2], 0).then_inc(S("ovf_turned", L), 1)

            def combine(L):
                pe.wait_ge(S("yT_ready"), L + 1)
                for f in range(2 * SB):
                    s, half = divmod(f, 2)
                    for mq in range(4):
                        last = nc.tensor.transpose(bank[f][:, mq * P:(mq + 1) * P],
                                                   yT[:, half * 4 + mq, s * P:(s + 1) * P], ident)
                    last.then_inc(S("yT_turned", L), 1)
                for half in range(2):
                    pe.wait_ge(S("yS_act" if half == 0 else "yS_dve", L), SB)
                    for t in range(T):
                        for s in range(SB):
                            last = mm(bank[half + 2 * t][:, :], pwT[:, s, t * P:(t + 1) * P],
                                      yS[:, s, half * 512:half * 512 + 512], s == 0, s == SB - 1)
                        last.then_inc(S("moe_out", L), 1)

            for a in range(4):
                bcast(a)
            gain(ROW_MIX, 6, "gain_mix_0")
            pe.wait_ge(S("h_ready"), nth(0, "mix") * T + T)
            pe.wait_ge(S("band_loaded"), 16)
            for m in range(KC):
                for t in range(T):
                    last = mm(bank[m // 2][:, (m % 2) * SEQ:(m % 2 + 1) * SEQ], h[:, t, m * P:(m + 1) * P],
                              band_sb[:, t, m // 2, :], t == 0, t == T - 1)
                if m % 2:
                    last.then_inc(S("pT_full"), 1)
            pe.wait_ge(S("A_ready", 0, "mix"), 2)
            gain(ROW_PS, 6, "gain_ps")
            pe.wait_ge(S("pT_ready"), 4)
            pe.wait_ge(S("ring_full", IT_POOL % R), full_at(IT_POOL))
            pw = cols_w(IT_POOL % R, SEQ)
            for half in range(2):
                for t in range(T):
                    for gg in range(2):
                        for cc in range(2):
                            m = (2 * half + gg) * 2 + cc
                            last = mm(bank[half + 2 * t][:, gg * SEQ:(gg + 1) * SEQ], pT[:, m, t * P:(t + 1) * P],
                                      pw[:, m, :], cc == 0, cc == 1)
                    last.then_inc(S("mix_out", 0), 1)
            pe.wait_ge(S("mix_out", 0), 2 * T)
            pe.sem_inc(S("ring_free", IT_POOL % R), 1)
            for a in range(4, 8):
                bcast(a)
            pe.wait_ge(S("ps_used"), 2)
            gain(ROW_FFN, 6, "gain_ffn_0")
            transposes(0, "ffn")
            route(0)
            gather(0)
            for e in range(R):
                expert_at(0, e)
            experts(0, R, HEAD_E)
            for a in range(8, 12):
                bcast(a)
            pe.wait_ge(S("pwT_ready"), 2)
            gain(ROW_MIX + 1, 6, "gain_mix_1")
            for e in range(HEAD_E, E):
                expert_at(0, e)
            turn_last(0, E, 1)
            overflow(0)
            pe.wait_ge(S("A_ready", 1, "mix"), 2)
            combine(0)

            transposes(1, "mix")
            pe.wait_ge(S("hT_act"), (nth(1, "mix") - 1) * 2 + 2)
            pe.wait_ge(S("hT_dve"), (nth(1, "mix") - 1) * 2 + 2)
            u = 0
            for j, n in enumerate(IT_QKV):
                pe.wait_ge(S("ring_full", n % R), full_at(n))
                w = cols_w(n % R, AC)
                for col in range(j * AC, (j + 1) * AC, P):
                    m = col // P
                    if m >= 16 and m % 2:
                        continue
                    for t in range(1 if m < 16 else T):
                        if u >= 4:
                            pe.wait_ge(S("qkv_read"), u - 3)
                        for k in range(KC):
                            c0 = col - j * AC
                            if m < 16:
                                last = mm(bank[u % 4][:, 0:SEQ], w[:, k, c0:c0 + P], hT[:, k, :], k == 0, k == KC - 1)
                            else:
                                last = mm(bank[u % 4][:, 0:SEQ], hT[:, k, t * P:(t + 1) * P], w[:, k, c0:c0 + 256],
                                          k == 0, k == KC - 1)
                        last.then_inc(S("qkv_full"), 1)
                        u += 1
                pe.wait_ge(S("qkv_full"), u)
                pe.sem_inc(S("ring_free", n % R), 1)
                if j >= 1:
                    bcast(12 + j - 1)
            pe.wait_ge(S("qkv_read"), u)
            pe.wait_ge(S("mod_written"), 2 * 15)

            def scores(m, a):
                for t in range(T):
                    last = mm(bank[4 + a][:, t * P:t * P + (t + 1) * P], qT[a * DH:(a + 1) * DH, m, t * P:(t + 1) * P],
                              kT[a * DH:(a + 1) * DH, m, 0:(t + 1) * P], True, True)
                last.then_inc(S("s_full"), 1)

            def turn(hd, a):
                pe.wait_ge(S("p_ready"), 2 * hd + 2)
                for s in range(3):
                    last = nc.tensor.transpose(bank[6 + a][:, s * P:(s + 1) * P], pr[a][:, s * P:(s + 1) * P], ident)
                last.then_inc(S("pT_turned"), 1)

            def weigh(hd, m, a):
                pe.wait_ge(S("prT_ready"), hd + 1)
                cols = slice(a * DH, (a + 1) * DH)
                o_ = bank[0][a * DH:(a + 1) * DH, :]
                vm = v[:, :, bass.ds(m * P + a * DH, DH)]
                mm(o_[:, 0:SEQ], vm[:, 0, :], prT[a][:, 0:SEQ], True, False)
                mm(o_[:, P:SEQ], vm[:, 1, :], prT[a][:, SEQ:3 * P], False, True).then_inc(S("pv_done"), 1)

            def q_of(m):
                return m

            scores(0, 0)
            scores(0, 1)
            for m in range(NH // 2):
                for a in range(2):
                    hd = 2 * m + a
                    if hd >= 2:
                        pe.wait_ge(S("prT_ready"), hd - 1)
                    turn(hd, a)
                    if hd >= 1:
                        pm, pa = divmod(hd - 1, 2)
                        if pa == 0 and pm >= 1:
                            pe.wait_ge(S("o_read"), pm)
                        weigh(hd - 1, pm, pa)
                    if hd + 2 < NH:
                        pe.wait_ge(S("s_read"), hd + 1)
                        scores(m + 1, a)
            weigh(NH - 1, NH // 2 - 1, 1)
            pe.wait_ge(S("s_read"), NH)
            bcast(15)
            pe.wait_ge(S("prT_ready"), NH)
            gain(ROW_FFN + 1, 6, "gain_ffn_1")
            pe.wait_ge(S("o_read"), NH // 2)
            for j, n in enumerate(IT_WO):
                pe.wait_ge(S("ring_full", n % R), full_at(n))
                w = cols_w(n % R, 512)
                for t in range(T):
                    for m in range(KC):
                        last = mm(bank[j + 2 * t][:, :], oT[:, m, t * P:(t + 1) * P], w[:, m, :], m == 0, m == KC - 1)
                    last.then_inc(S("mix_out", 1), 1)
                pe.wait_ge(S("mix_out", 1), T * (j + 1))
                pe.sem_inc(S("ring_free", n % R), 1)
            transposes(1, "ffn")
            route(1)
            gather(1)
            for e in range(R):
                expert_at(1, e)
            experts(1, R, E)
            turn_last(1, E, 1)
            overflow(1)
            pe.wait_ge(S("pwT_ready"), 2 + 2)
            combine(1)
            gain(ROW_FIN, 4, "gain_fin")

        @block.scalar
        def _(act):
            act.dma_start(ccol[:, :], c.rearrange("b (p k) -> (b p) k", k=KC)).then_inc(S("c_loaded"), 16)
            act.dma_start(cst[:, :], misc).then_inc(S("misc_loaded"), 16)
            for L in range(2):
                act.dma_start(rows[ROW_B[L]:ROW_B[L] + 6, :], ada_b[L].rearrange("(a d) -> a d", a=6))\
                    .then_inc(S("rows_loaded"), 16)
            act.dma_start(rows[ROW_MIX:ROW_MIX + 2, :], norm_mix_g).then_inc(S("rows_loaded"), 16)
            act.dma_start(rows[ROW_FFN:ROW_FFN + 2, :], norm_ffn_g).then_inc(S("rows_loaded"), 16)
            act.dma_start(rows[ROW_PS:ROW_PS + 1, :], pool_scale).then_inc(S("rows_loaded"), 16)
            act.dma_start(rows[ROW_FIN:ROW_FIN + 1, :], final_norm_g.rearrange("(a d) -> a d", a=1))\
                .then_inc(S("rows_loaded"), 16)
            act.dma_start(x_sb[:, :, :], x_d).then_inc(S("x_loaded"), 16)
            act.dma_start(band_sb, band.rearrange("p (t g q) -> p t g q", t=T, g=NG)).then_inc(S("band_loaded"), 16)
            act.dma_start(stage_g, router_group_w.rearrange("l (p k) n -> p l k n", k=KC)).then_inc(S("stage_loaded"), 16)
            act.dma_start(stage_e, router_expert_w.rearrange("l (p k) n -> p l k n", k=KC)).then_inc(S("stage_loaded"), 16)

            def copy(o_, i_):
                return nc.scalar.activation(o_, i_, ACT.Identity)

            def squares(L, w, waits, dump=reg_h):
                for t in range(T):
                    act.wait_ge(*waits(t))
                    nc.scalar.activation(dump[:, t * D:(t + 1) * D], x_sb[:, t, :], ACT.Square, accum_out=ss[:, t:t + 1])\
                        .then_inc(S("ss_ready"), 1)

            def root(L, w):
                act.wait_ge(S("ms_ready"), nth(L, w) * 1 + 1)
                nc.scalar.activation(rt[:, :], ms[:, :], ACT.Sqrt).then_inc(S("rt_ready"), 1)

            def write_mod(a):
                for b, (lo, hi) in enumerate(pieces(a % 8)):
                    act.wait_ge(S("bcast_ready"), 2 * a + b + 1)
                    copy(mod[:, lo:hi], bank[4 + b][:, 0:hi - lo]).then_inc(S("mod_written"), 1)

            def evac_hT(L, w):
                for b in (0, 2):
                    act.wait_ge(S("hT_full"), (nth(L, w) - 1) * 4 + b + 1)
                    copy(hT[:, 2 * b:2 * b + 2, :], bank[b][:, :].rearrange("p (k q) -> p k q", k=2))\
                        .then_inc(S("hT_act"), 1)

            def route(L):
                act.wait_ge(S("gd_ready"), L + 1)
                nc.scalar.activation(gd[:, :, :], gd[:, :, :], ACT.Exp).then_inc(S("gexp"), 1)
                act.wait_ge(S("ed_ready"), L + 1)
                nc.scalar.activation(ed[:, :, :], ed[:, :, :], ACT.Exp).then_inc(S("gexp"), 1)

            def evac_gather(L):
                for k in range(KC):
                    act.wait_ge(S("gathered"), L * KC + k + 1)
                    last = copy(hS[:, k, 0:NSLOT], bank[k % 4][:, :])
                    last.then_inc(S("hS_ready"), 1)
                for b in range(2):
                    act.wait_ge(S("pwT_full"), L * 2 + b + 1)
                    copy(pwT[:, 2 * b:2 * b + 2, :], bank[6 + b][:, :].rearrange("p (s q) -> p s q", s=2))\
                        .then_inc(S("pwT_ready"), 1)
                act.wait_ge(S("hS_ready"), L * KC + KC)
                act.sem_inc(S("heT_ready", L), 2)
                act.sem_inc(S("dn_free", L), 2)

            def silu(L, e, b):
                act.wait_ge(S("gu_ready", L), e + 1)
                nc.scalar.activation(sil[:, b, :], bank[b][:, 0:P], ACT.Silu).then_inc(S("sil_ready", L), 1)

            def yT_at(off):
                return yT[:, :, bass.ds(off, CAP)]

            def from_turned(b):
                return b[:, :].rearrange("p (m s) -> p m s", m=KC)

            def put_y(L, e, b):
                off = act.value_load(off_i[0:1, L, bass.ds(e, 1)], min_val=0, max_val=NSLOT)
                act.wait_ge(S("ye_turned", L), e + 1)
                act.wait_ge(S("dn_free", L), e + 2)
                copy(yT_at(off), from_turned(bank[2 + b])).then_inc(S("dn_free", L), 1)

            def experts(L, e0, e1):
                with act.Fori(0, (e1 - e0) // R) as i:
                    for u in range(R):
                        silu(L, i * R + (e0 + u), u % 2)
                        put_y(L, i * R + (e0 + u - 1), 1 - u % 2)

            def expert_at(L, e):
                silu(L, e, e % 2)
                if e:
                    put_y(L, e - 1, 1 - e % 2)

            def overflow(L):
                n_ovf = act.value_load(ov_i[0:1, L, 2 * MAXOVF:2 * MAXOVF + 1], min_val=0, max_val=MAXOVF)
                with act.If(n_ovf > 0):
                    with act.Fori(0, n_ovf) as i:
                        e = act.value_load(ov_i[0:1, L, bass.ds(i, 1)], min_val=0, max_val=E - 1)
                        off = act.value_load(ov_i[0:1, L, bass.ds(i + MAXOVF, 1)], min_val=0, max_val=NSLOT)
                        act.wait_ge(S("ovf_pe", L), i * 3)
                        act.dma_start(reg_h[:, :], gate_d[L][bass.ds(e, 1), :, :].rearrange("a p n -> (a p) n"))\
                            .then_inc(S("ovf_w", L), 16)
                        act.wait_ge(S("ovf_pe", L), i * 3 + 1)
                        act.dma_start(reg_h[:, :], up_d[L][bass.ds(e, 1), :, :].rearrange("a p n -> (a p) n"))\
                            .then_inc(S("ovf_w", L), 16)
                        act.wait_ge(S("ovf_pe", L), i * 3 + 2)
                        act.dma_start(reg_h[:, :].rearrange("p (j d) -> p j d", j=2),
                                      down_d[L][bass.ds(e, 1), :, :, :].rearrange("a p j d -> (a p) j d"))\
                            .then_inc(S("ovf_w", L), 16)
                        nc.scalar.activation(sil[:, 0, :], bank[0][:, 0:P], ACT.Silu).then_inc(S("ovf_sil", L), 1)
                        act.wait_ge(S("ovf_turned", L), i + 1)
                        copy(yT_at(off), from_turned(bank[2])).then_inc(S("ovf_y", L), 1)
                        act.wait_ge(S("ovf_y", L), i + 1)
                act.wait_ge(S("dn_free", L), E + 2)
                act.sem_inc(S("yT_ready"), 1)

            def evac_yT(L):
                for f in range(0, 2 * SB, 2):
                    act.wait_ge(S("yT_turned", L), f + 1)
                    copy(yS[:, f // 2, 0:512], bank[f][:, :]).then_inc(S("yS_act", L), 1)

            act.wait_ge(S("c_loaded"), 16)
            nc.scalar.activation(cact[:, :], ccol[:, :], ACT.Silu).then_inc(S("cact_ready"), 1)
            squares(0, "mix", lambda t: (S("x_loaded"), 16))
            for a in range(4):
                write_mod(a)
            root(0, "mix")
            for b in range(4):
                act.wait_ge(S("pT_full"), b + 1)
                copy(pT[:, 2 * b:2 * b + 2, :], bank[b][:, :].rearrange("p (m q) -> p m q", m=2))\
                    .then_inc(S("pT_ready"), 1)
            for a in range(4, 8):
                write_mod(a)
            squares(0, "ffn", lambda t: (S("x_mixed", 0), 2 + t + 1))
            root(0, "ffn")
            evac_hT(0, "ffn")
            route(0)
            evac_gather(0)
            for e in range(R):
                expert_at(0, e)
            experts(0, R, HEAD_E)
            for a in range(8, 12):
                write_mod(a)
            for e in range(HEAD_E, E):
                expert_at(0, e)
            put_y(0, E - 1, 1)
            overflow(0)
            evac_yT(0)
            squares(1, "mix", lambda t: (S("x_moe", 0), 2 + t + 1))
            root(1, "mix")
            evac_hT(1, "mix")
            u = 0
            for j in range(4):
                for m in range(6 * j, 6 * j + 6):
                    if m >= 16 and m % 2:
                        continue
                    for t in range(1 if m < 16 else T):
                        act.wait_ge(S("qkv_full"), u + 1)
                        src = bank[u % 4][:, 0:SEQ]
                        if m < 8:
                            last = nc.scalar.activation(qT[:, m, :], src, ACT.Identity, scale=DH ** -0.5)
                        elif m < 16:
                            last = copy(kT[:, m - 8, :], src)
                        else:
                            last = copy(v[:, t, (m - 16) * P:(m - 14) * P], src)
                        last.then_inc(S("qkv_read"), 1)
                        u += 1
                if j >= 1:
                    write_mod(12 + j - 1)

            def exps(hd, a):
                act.wait_ge(S("mx_ready"), 2 * hd + 2)
                if hd >= 2:
                    act.wait_ge(S("pT_turned"), hd - 1)
                for t in range(T):
                    cols = slice(t * P, t * P + (t + 1) * P)
                    nc.scalar.activation(pr[a][:, cols], sc[a][:, cols], ACT.Exp, bias=nmx[:, a, t:t + 1],
                                         accum_out=psm[:, a, t:t + 1]).then_inc(S("exp_done"), 1)

            def evac_prT(hd, a):
                act.wait_ge(S("pT_turned"), hd + 1)
                if hd >= 2:
                    act.wait_ge(S("pv_done"), hd - 1)
                copy(prT[a], bank[6 + a][:, 0:3 * P]).then_inc(S("prT_ready"), 1)

            for hd in range(NH):
                exps(hd, hd % 2)
                if hd:
                    evac_prT(hd - 1, (hd - 1) % 2)
            evac_prT(NH - 1, 1)
            write_mod(15)
            squares(1, "ffn", lambda t: (S("x_mixed", 1), 2 + t + 1), dump=reg_b)
            root(1, "ffn")
            evac_hT(1, "ffn")
            route(1)
            evac_gather(1)
            for e in range(R):
                expert_at(1, e)
            experts(1, R, E)
            put_y(1, E - 1, 1)
            overflow(1)
            evac_yT(1)
            squares(2, "fin", lambda t: (S("x_moe", 1), 2 + t + 1))
            root(2, "fin")

        @block.vector
        def _(dve):
            steps = [0]

            def then(ins):
                steps[0] += 1
                ins.then_inc(S("dve_step"), 1)
                dve.wait_ge(S("dve_step"), steps[0])

            def tt(o_, a_, b_, op):
                return nc.vector.tensor_tensor(o_, a_, b_, op)

            def stt(o_, a_, s_, b_, op0, op1):
                return nc.vector.scalar_tensor_tensor(o_, a_, s_, b_, op0, op1)

            def ada(a):
                n = IT_ADA[a]
                w = cols_w(n % R, AC)
                dve.wait_ge(S("ring_full", n % R), full_at(n))
                if a == 0:
                    dve.wait_ge(S("cact_ready"), 1)
                if a >= 2:
                    dve.wait_ge(S("bcast_ready"), 2 * (a - 1))
                for k in range(KC):
                    for hf in range(2):
                        cols = slice(hf * AC // 2, (hf + 1) * AC // 2)
                        dst = acc[:, a % 2, cols]
                        if k == 0:
                            ins = nc.vector.tensor_scalar(dst, w[:, k, cols], cact[:, k:k + 1], None, ALU.mult)
                        else:
                            dve.wait_ge(S("acc_step"), 2 * (KC - 1) * a + 2 * (k - 1) + hf + 1)
                            ins = stt(dst, w[:, k, cols], cact[:, k:k + 1], dst, ALU.mult, ALU.add)
                        if k < KC - 1:
                            ins.then_inc(S("acc_step"), 1)
                        else:
                            ins.then_inc(S("acc_ready"), 1)
                dve.wait_ge(S("acc_ready"), 2 * (a + 1))
                dve.sem_inc(S("ring_free", n % R), 1)

            def scale_vec(L, w, j, name):
                dve.wait_ge(S("mod_written"), 2 * (8 * L + 4 + (4 if w == "ffn" else 0)))
                for b in range(2):
                    dve.wait_ge(S(name), b + 1)
                    cols = slice(j * D + b * 512, j * D + b * 512 + 512)
                    stt(mod[:, cols], mod[:, cols], 1.0, bank[6 + b][:, :], ALU.add, ALU.mult)\
                        .then_inc(S("A_ready", L, w), 1)
                dve.wait_ge(S("A_ready", L, w), 2)

            def rstd(L, w):
                dve.wait_ge(S("ss_ready"), nth(L, w) * T + T)
                nc.vector.tensor_scalar(ms[:, :], ss[:, :], 1.0 / D, EPS, ALU.mult, ALU.add)\
                    .then_inc(S("ms_ready"), 1)
                dve.wait_ge(S("rt_ready"), nth(L, w) * 1 + 1)
                then(nc.vector.reciprocal(rs[:, :], rt[:, :]))

            def norm(L, w, ja, jb):
                for t in range(T):
                    stt(h[:, t, :], x_sb[:, t, :], rs[:, t:t + 1], mod[:, ja * D:(ja + 1) * D], ALU.mult, ALU.mult)\
                        .then_inc(S("h_scaled"), 1)
                for t in range(T):
                    dve.wait_ge(S("h_scaled"), nth(L, w) * T + t + 1)
                    tt(h[:, t, :], h[:, t, :], mod[:, jb * D:(jb + 1) * D], ALU.add).then_inc(S("h_ready"), 1)

            def add_to_x(ready, done, jg, tmp):
                for half in range(2):
                    cols = slice(half * 512, half * 512 + 512)
                    for t in range(T):
                        dve.wait_ge(ready, half * T + t + 1)
                        then(tt(tmp, bank[half + 2 * t][:, :], mod[:, jg * D + half * 512:jg * D + half * 512 + 512], ALU.mult))
                        tt(x_sb[:, t, cols], x_sb[:, t, cols], tmp, ALU.add).then_inc(done, 1)
                        dve.wait_ge(done, half * T + t + 1)

            def evac_hT(L, w):
                for b in (1, 3):
                    dve.wait_ge(S("hT_full"), (nth(L, w) - 1) * 4 + b + 1)
                    nc.vector.tensor_copy(hT[:, 2 * b:2 * b + 2, :], bank[b][:, :].rearrange("p (k q) -> p k q", k=2))\
                        .then_inc(S("hT_dve"), 1)

            def wide(ap, n):
                return ap.broadcast_to([P, T, n])

            def first_max(val, mx, n, oh, eq, cm):
                then(nc.vector.tensor_reduce(mx, val, AX, ALU.max))
                then(tt(eq, val, wide(mx, n), ALU.is_equal))
                then(tt(eq, eq, first8[:, EPG - n:EPG].unsqueeze(1).broadcast_to([P, T, n]), ALU.mult))
                then(nc.vector.tensor_reduce(cm, eq, AX, ALU.max))
                then(tt(oh, eq, wide(cm, n), ALU.is_equal))

            def route(L):
                dve.wait_ge(S("logits"), L + 1)
                then(nc.vector.tensor_copy(lg[:, :, :], bank[4][:, 0:T * 36].rearrange("p (t n) -> p t n", t=T)))
                first_max(lg[:, :, 0:NG], gm[:, :, :], NG, goh[:, :, :], geq[:, :, :], ecm[:, :, :])
                tt(gd[:, :, :], lg[:, :, 0:NG], wide(gm[:, :, :], NG), ALU.subtract).then_inc(S("gd_ready"), 1)
                el = lg[:, :, NG:NG + E].rearrange("p t (g j) -> p t g j", g=NG)
                for t in range(T):
                    last = tt(prod[:, t, :, :], el[:, t, :, :],
                              goh[:, t, :].unsqueeze(2).broadcast_to([P, NG, EPG]), ALU.mult)
                then(last)
                then(nc.vector.tensor_reduce(se[0][:, :, :], prod[:, :, :, :].rearrange("p t g j -> p t j g"), AX, ALU.add))
                first_max(se[0][:, :, :], emx[0][:, :, :], EPG, eoh[0][:, :, :], eeq[:, :, :], ecm[:, :, :])
                then(stt(se[1][:, :, :], eoh[0][:, :, :], -BIG, se[0][:, :, :], ALU.mult, ALU.add))
                first_max(se[1][:, :, :], emx[1][:, :, :], EPG, eoh[1][:, :, :], eeq[:, :, :], ecm[:, :, :])
                tt(ed[:, :, :], emx[1][:, :, :], emx[0][:, :, :], ALU.subtract).then_inc(S("ed_ready"), 1)
                for i in range(2):
                    for t in range(T):
                        last = tt(msk[i][:, t, :].rearrange("p (g j) -> p g j", g=NG),
                                  goh[:, t, :].unsqueeze(2).broadcast_to([P, NG, EPG]),
                                  eoh[i][:, t, :].unsqueeze(1).broadcast_to([P, NG, EPG]), ALU.mult)
                then(last)
                tt(mask[:, :, :], msk[0][:, :, :], msk[1][:, :, :], ALU.add).then_inc(S("mask_ready"), 1)
                dve.wait_ge(S("gexp"), L * 2 + 2)
                then(nc.vector.tensor_reduce(gsum[:, :, :], gd[:, :, :], AX, ALU.add))
                then(nc.vector.tensor_scalar(eden[:, :, :], ed[:, :, :], 1.0, None, ALU.add))
                then(tt(eden[:, :, :], eden[:, :, :], gsum[:, :, :], ALU.mult))
                then(nc.vector.reciprocal(wk[0][:, :, :], eden[:, :, :]))
                then(tt(wk[1][:, :, :], wk[0][:, :, :], ed[:, :, :], ALU.mult))
                dve.wait_ge(S("counts"), L + 1)
                then(nc.vector.tensor_copy(cnt[:, :], bank[5][:, 0:E]))
                then(nc.vector.tensor_tensor_scan(endc[:, :], cnt[:, :], cnt[:, :], 0.0, ALU.add, ALU.bypass)
                     if False else nc.vector.tensor_tensor_scan(endc[:, :], ones[:, 0:E], cnt[:, :], 0.0, ALU.mult, ALU.add))
                then(tt(offc[:, :], endc[:, :], cnt[:, :], ALU.subtract))
                nc.vector.tensor_copy(off_i[:, L, :], offc[0:1, :]).then_inc(S("off_ready"), 1)
                then(tt(posn[:, :, :], bank[5][:, E:3 * E].rearrange("p (t n) -> p t n", t=T),
                        offc[:, :].unsqueeze(1).broadcast_to([P, T, E]), ALU.add))
                for i in range(2):
                    then(tt(msk[i][:, :, :], msk[i][:, :, :], posn[:, :, :], ALU.mult))
                    then(nc.vector.tensor_reduce(slot_of[i][:, :, :], msk[i][:, :, :], AX, ALU.add))
                for t in range(T):
                    then(nc.vector.tensor_scalar(pick[:, t, :], iota, slot_of[0][:, t, :], None, ALU.is_equal))
                    stt(pick[:, t, :], iota, slot_of[1][:, t, :], pick[:, t, :], ALU.is_equal, ALU.add)\
                        .then_inc(S("pick_ready"), 1)
                if L == 0:
                    dve.wait_ge(S("rw_ready"), 2)
                for t in range(T):
                    tmp = reg_c[:, 1024:1024 + NSLOT]
                    then(nc.vector.tensor_scalar(pickw[:, t, :], iota, slot_of[0][:, t, :], wk[0][:, t, :],
                                                 ALU.is_equal, ALU.mult))
                    then(nc.vector.tensor_scalar(tmp, iota, slot_of[1][:, t, :], wk[1][:, t, :],
                                                 ALU.is_equal, ALU.mult))
                    tt(pickw[:, t, :], pickw[:, t, :], tmp, ALU.add).then_inc(S("pickw_ready"), 1)
                    dve.wait_ge(S("pickw_ready"), L * T + t + 1)
                nc.vector.memset(hS[:, :, NSLOT:PAD], 0.0).then_inc(S("hS_pad"), 1)
                overflow_list()
                ins = nc.vector.tensor_copy(ov_i[:, L, :], ov_f[:, :])
                ins.then_inc(S("ovf_ready"), 1)

            def overflow_list():
                n1, end1, off1 = cnt[0:1, :], endc[0:1, :], offc[0:1, :]
                for q in range(NC_):
                    then(nc.vector.tensor_scalar(ov_ind[:, q, :], n1, float(CAP * (q + 1)), None, ALU.is_gt))
                then(nc.vector.tensor_reduce(ov_n[:, :], ov_ind[:, :, :].rearrange("p q e -> p e q"), AX, ALU.add))
                then(nc.vector.tensor_tensor_scan(ov_end[:, :], ones[0:1, 0:E], ov_n[:, :], 0.0, ALU.mult, ALU.add))
                then(tt(ov_n[:, :], ov_end[:, :], ov_n[:, :], ALU.subtract))
                then(nc.vector.tensor_scalar(ov_last[:, :], end1, -float(CAP), None, ALU.add))
                for q in range(NC_):
                    then(nc.vector.tensor_scalar(ov_rank[:, q, :], ov_n[:, :], float(q), None, ALU.add))
                    then(stt(ov_start[:, q, :], off1, float(CAP * (q + 1)), ov_last[:, :], ALU.add, ALU.min))
                for i in range(MAXOVF):
                    then(stt(ov_tmp[:, :, :], ov_rank[:, :, :], float(i), ov_ind[:, :, :], ALU.is_equal, ALU.mult))
                    then(nc.vector.tensor_tensor_reduce(
                        ov_dump[:, :, :], ov_tmp[:, :, :], iota[0:1, 0:E].unsqueeze(1).broadcast_to([1, NC_, E]),
                        1.0, 0.0, ALU.mult, ALU.add, ov_f[:, i:i + 1]))
                    then(nc.vector.tensor_tensor_reduce(
                        ov_dump[:, :, :], ov_tmp[:, :, :], ov_start[:, :, :],
                        1.0, 0.0, ALU.mult, ALU.add, ov_f[:, MAXOVF + i:MAXOVF + i + 1]))
                then(nc.vector.tensor_copy(ov_f[:, 2 * MAXOVF:2 * MAXOVF + 1], ov_end[:, E - 1:E]))

            def expert(L, e, b, s):
                dve.wait_ge(S("gu_ready", L), e + 1)
                dve.wait_ge(S("sil_ready", L), e + 1)
                tt(he[:, b, :], sil[:, b, :], bank[b][:, P:2 * P], ALU.mult).then_inc(S("he_ready", L), 1)
                dve.wait_ge(S("he_turned", L), e + 1)
                nc.vector.tensor_copy(heT[:, b, :], bank[b][:, 2 * P:3 * P]).then_inc(S("heT_ready", L), 1)
                dve.wait_ge(S("dn_ready", L), e + 1)
                dve.sem_inc(S("ring_free", s), 1)
                nc.vector.tensor_copy(ye[:, b, :], bank[2 + b][:, :]).then_inc(S("ye_ready", L), 1)

            def experts(L, e0, e1):
                n0 = IT_EXP[L](e0)
                with dve.Fori(0, (e1 - e0) // R) as i:
                    for u in range(R):
                        expert(L, i * R + (e0 + u), u % 2, (n0 + u) % R)

            def expert_at(L, e):
                expert(L, e, e % 2, IT_EXP[L](e) % R)

            def overflow(L):
                n_ovf = dve.value_load(ov_i[0:1, L, 2 * MAXOVF:2 * MAXOVF + 1], min_val=0, max_val=MAXOVF)
                with dve.If(n_ovf > 0):
                    with dve.Fori(0, n_ovf) as i:
                        dve.wait_ge(S("ovf_sil", L), i + 1)
                        tt(he[:, 0, :], sil[:, 0, :], bank[0][:, P:2 * P], ALU.mult).then_inc(S("ovf_he", L), 1)
                        dve.wait_ge(S("ovf_he_turned", L), i + 1)
                        nc.vector.tensor_copy(heT[:, 0, :], bank[0][:, 2 * P:3 * P]).then_inc(S("ovf_heT", L), 1)
                        dve.wait_ge(S("ovf_pe", L), i * 3 + 3)
                        nc.vector.tensor_copy(ye[:, 0, :], bank[2][:, :]).then_inc(S("ovf_ye", L), 1)

            def evac_yT(L):
                for f in range(1, 2 * SB, 2):
                    dve.wait_ge(S("yT_turned", L), f + 1)
                    nc.vector.tensor_copy(yS[:, f // 2, 512:D], bank[f][:, :]).then_inc(S("yS_dve", L), 1)

            for a in range(4):
                ada(a)
            scale_vec(0, "mix", 1, "gain_mix_0")
            rstd(0, "mix")
            norm(0, "mix", 1, 0)
            ada(4)
            for b in range(2):
                dve.wait_ge(S("gain_ps"), b + 1)
                cols = slice(2 * D + b * 512, 2 * D + b * 512 + 512)
                tt(mod[:, cols], mod[:, cols], bank[6 + b][:, :], ALU.mult).then_inc(S("ps_used"), 1)
            dve.wait_ge(S("ps_used"), 2)
            ada(5)
            add_to_x(S("mix_out", 0), S("x_mixed", 0), 2, reg_b[:, 0:512])
            ada(6)
            ada(7)
            scale_vec(0, "ffn", 4, "gain_ffn_0")
            rstd(0, "ffn")
            norm(0, "ffn", 4, 3)
            evac_hT(0, "ffn")
            route(0)
            for e in range(R):
                expert_at(0, e)
            experts(0, R, HEAD_E)
            for a in range(8, 12):
                ada(a)
            scale_vec(1, "mix", 1, "gain_mix_1")
            for e in range(HEAD_E, E):
                expert_at(0, e)
            overflow(0)
            evac_yT(0)
            add_to_x(S("moe_out", 0), S("x_moe", 0), 5, reg_c[:, 1024:1536])

            rstd(1, "mix")
            norm(1, "mix", 1, 0)
            evac_hT(1, "mix")
            for a in range(12, 16):
                ada(a)

            def front(hd, a):
                dve.wait_ge(S("s_full"), hd + 1)
                if hd >= 2:
                    dve.wait_ge(S("exp_done"), 2 * hd - 2)
                stt(sc[a], alibi, slopes[:, hd:hd + 1], bank[4 + a][:, 0:3 * P], ALU.mult, ALU.add)\
                    .then_inc(S("s_read"), 1)
                dve.wait_ge(S("s_read"), hd + 1)
                for t in range(T):
                    nc.vector.tensor_reduce(nmx[:, a, t:t + 1], sc[a][:, t * P:t * P + (t + 1) * P], AX, ALU.max,
                                            negate=True).then_inc(S("mx_ready"), 1)

            def back(hd, a):
                dve.wait_ge(S("exp_done"), 2 * hd + 2)
                then(nc.vector.reciprocal(prc[:, a, :], psm[:, a, :]))
                for t in range(T):
                    cols = slice(t * P, t * P + (t + 1) * P)
                    nc.vector.tensor_scalar(pr[a][:, cols], pr[a][:, cols], prc[:, a, t:t + 1], None, ALU.mult)\
                        .then_inc(S("p_ready"), 1)

            def evac_o(m):
                dve.wait_ge(S("pv_done"), 2 * m + 2)
                nc.vector.tensor_copy(oT[:, m, :], bank[0][:, 0:SEQ]).then_inc(S("o_read"), 1)

            front(0, 0)
            for hd in range(NH):
                if hd + 1 < NH:
                    front(hd + 1, (hd + 1) % 2)
                back(hd, hd % 2)
                if hd >= 3 and hd % 2:
                    evac_o((hd - 3) // 2)
            evac_o(NH // 2 - 1)
            scale_vec(1, "ffn", 4, "gain_ffn_1")
            add_to_x(S("mix_out", 1), S("x_mixed", 1), 2, reg_a[:, 0:512])
            rstd(1, "ffn")
            norm(1, "ffn", 4, 3)
            evac_hT(1, "ffn")
            route(1)
            for e in range(R):
                expert_at(1, e)
            experts(1, R, E)
            overflow(1)
            evac_yT(1)
            add_to_x(S("moe_out", 1), S("x_moe", 1), 5, reg_c[:, 1024:1536])
            rstd(2, "fin")
            for t in range(T):
                for b in range(2):
                    dve.wait_ge(S("gain_fin"), b + 1)
                    cols = slice(b * 512, b * 512 + 512)
                    last = stt(h[:, t, cols], x_sb[:, t, cols], rs[:, t:t + 1], bank[4 + b][:, :], ALU.mult, ALU.mult)
                last.then_inc(S("result_ready"), 1)


_INS = ["x", "c", "ada_w", "ada_b", "norm_mix_g", "norm_ffn_g", "pool_w", "pool_scale", "w_qkv", "w_o",
        "router_group_w", "router_expert_w", "exp_w_gate", "exp_w_up", "exp_w_down", "final_norm_g"]


def kernel(**inputs):
    import numpy as _np
    import concourse.bacc as _bacc
    from concourse import mybir as _mybir
    from concourse.bass_utils import run_bass_kernel_spmd as _run

    nc = _bacc.Bacc("TRN2", target_bir_lowering=False, num_devices=1)
    arrays, args = {}, {}
    for name, a in [(n, inputs[n]) for n in _INS] + list(constants().items()):
        a = _np.ascontiguousarray(a)
        arrays[f"in_{name}_dram"] = a
        args[name] = nc.dram_tensor(f"in_{name}_dram", a.shape, _mybir.dt.from_np(a.dtype), kind="ExternalInput").ap()
    out = nc.dram_tensor("out_0_dram", (1, SEQ, D), _mybir.dt.float32, kind="ExternalOutput").ap()
    program(nc, **args, out=out)
    r = _run(nc, [arrays], core_ids=[0])
    return r.results[0]["out_0_dram"]
```

```python
from contextlib import ExitStack

import numpy as np

import concourse.bass as bass
from concourse import mybir

P = 128
SEQ, D, F, E = 256, 1024, 256, 32
NG, EPG, TOPK = 4, 8, 2
NH, DH = 16, 64
T = SEQ // P
KC = D // P
NSLOT = SEQ * TOPK
SB = NSLOT // P
CAP = 64
PAD = NSLOT + CAP
MAXOVF = NSLOT // CAP - 1
R = 4
STAGES = (20, 24, 28)
SLOT = 3 * D * F // P
AC = SLOT // KC
WINDOWS = (2, 4, 8, 16)
EPS = 1e-6
BIG = 3.0e38
MASKED = -1.0e30

ALU = mybir.AluOpType
ACT = mybir.ActivationFunctionType
F32 = mybir.dt.float32
I32 = mybir.dt.int32
AX = mybir.AxisListType.X

IT_ADA = [0, 1, 2, 3, 5, 6, 7, 8] + [9, 10, 11, 16, 45, 47, 50, 52]
IT_POOL = 4
IT_EXP = [lambda e: 12 + e if e < R else 13 + e, lambda e: 55 + e]
ADA_PE = 12

IT_QKV = [46, 48, 49, 51]
IT_WO = [53, 54]

ROW_B = [0, 6]
ROW_MIX, ROW_PS, ROW_FIN = 12, 13, 14
NROWS = 15


def constants():
    ident = np.eye(P, dtype=np.float32)
    tri = np.triu(np.ones((P, P), np.float32), 1)
    iota = np.broadcast_to(np.arange(NSLOT, dtype=np.float32), (P, NSLOT)).copy()
    pos = np.arange(SEQ)
    band = np.zeros((SEQ, len(WINDOWS), SEQ), np.float32)
    for g, w in enumerate(WINDOWS):
        inside = (pos[:, None] <= pos[None, :]) & (pos[:, None] > pos[None, :] - w)
        band[:, g] = inside / np.minimum(pos + 1, w)[None, :] - np.eye(SEQ)
    band = np.ascontiguousarray(band.reshape(T, P, -1).transpose(1, 0, 2).reshape(P, -1).astype(np.float32))
    dist = pos[:, None] - pos[None, :]
    alibi = np.where(dist >= 0, -dist, MASKED).astype(np.float32)
    alibi = np.concatenate([alibi[:P, :P], alibi[P:, :]], 1)
    slopes = np.broadcast_to((2.0 ** (-8.0 * np.arange(1, NH + 1) / NH)).astype(np.float32), (P, NH)).copy()
    first8 = np.broadcast_to(np.arange(EPG, 0, -1, dtype=np.float32), (P, EPG)).copy()
    quarter = (np.arange(P) % 32 == 0).astype(np.float32)[:, None]
    misc = np.concatenate([ident, tri, iota, alibi, slopes, first8, quarter], 1)
    return {"misc": np.ascontiguousarray(misc), "band": band}


def program(nc, x, c, ada_w, ada_b, norm_mix_g, norm_ffn_g, pool_w, pool_scale, w_qkv, w_o,
            router_group_w, router_expert_w, exp_w_gate, exp_w_up, exp_w_down, final_norm_g, misc, band, out):
    ctx = ExitStack()
    with ctx:
        def sb(name, shape, dt=F32):
            return ctx.enter_context(nc.sbuf_tensor(name, shape, dt))

        sems = {}

        def S(*name):
            key = "_".join(map(str, name))
            if key not in sems:
                sems[key] = ctx.enter_context(nc.semaphore(key))
            return sems[key]

        x_sb = sb("x_sb", [P, T, D])
        mod = sb("mod", [P, 6 * D])
        NM = 2 * P + NSLOT + 3 * P + NH + EPG + 1
        cst = sb("cst", [P, NM])
        ident, tri = cst[:, 0:P], cst[:, P:2 * P]
        iota = cst[:, 2 * P:2 * P + NSLOT]
        o = 2 * P + NSLOT
        alibi, slopes, first8 = cst[:, o:o + 3 * P], cst[:, o + 3 * P:o + 3 * P + NH], cst[:, o + 3 * P + NH:NM - 1]
        quarter = cst[:, NM - 1:NM].broadcast_to([P, P])
        ones = sb("ones", [P, P])
        rows = sb("rows", [NROWS, D])
        ccol = sb("ccol", [P, KC])
        cact = sb("cact", [P, KC])
        acc = sb("acc", [P, 2, AC])
        ring = sb("ring", [P, R, SLOT])
        rw = sb("rw", [P, 2, KC, NG + E])
        reg_h = sb("reg_h", [P, T * D])
        reg_a = sb("reg_a", [P, KC * PAD])
        reg_b = sb("reg_b", [P, KC * PAD])
        reg_c = sb("reg_c", [P, 15 * P])

        h = reg_h[:, :].rearrange("p (t d) -> p t d", t=T)
        h_str = reg_h[:, :].rearrange("p (t q k) -> p t k q", t=T, k=KC)
        h_of = [h, h, reg_a[:, 0:T * D].rearrange("p (t d) -> p t d", t=T), h,
                reg_a[:, 0:T * D].rearrange("p (t d) -> p t d", t=T)]
        hT_bank = [None, 0, 0, 4]
        hT = reg_b[:, 0:KC * SEQ].rearrange("p (k q) -> p k q", k=KC)
        band_sb = reg_a[:, 0:T * NG * SEQ].rearrange("p (t g q) -> p t g q", t=T, g=NG)
        pT = reg_a[:, 2048:2048 + KC * SEQ].rearrange("p (m q) -> p m q", m=KC)
        hS = reg_a[:, :].rearrange("p (k s) -> p k s", k=KC)
        yS = [mod[:, 3 * D:4 * D], mod[:, 4 * D:5 * D], reg_h[:, 0:D], reg_h[:, D:2 * D]]
        yT = reg_b[:, :].rearrange("p (m s) -> p m s", m=KC)
        pick = reg_b[:, 2048:2048 + T * NSLOT].rearrange("p (t s) -> p t s", t=T)
        pickw = reg_b[:, 3072:3072 + T * NSLOT].rearrange("p (t s) -> p t s", t=T)
        pwT = reg_c[:, 0:SB * SEQ].rearrange("p (s q) -> p s q", s=SB)
        stage_g = reg_c[:, 0:2 * KC * NG].rearrange("p (l k n) -> p l k n", l=2, k=KC)
        stage_e = reg_c[:, 64:64 + 2 * KC * E].rearrange("p (l k n) -> p l k n", l=2, k=KC)
        qT = reg_a[:, 0:2048].rearrange("p (m q) -> p m q", m=KC)
        kT = reg_a[:, 2048:4096].rearrange("p (m q) -> p m q", m=KC)
        oT = qT
        v = reg_b[:, 2048:4096].rearrange("p (t d) -> p t d", t=T)
        sc = [[reg_c[:, 3 * P * (2 * b + a):3 * P * (2 * b + a + 1)] for a in range(2)] for b in range(2)]
        prT = [[reg_b[:, 3 * P * (2 * b + a):3 * P * (2 * b + a + 1)] for a in range(2)] for b in range(2)]

        ss = sb("ss", [P, T])
        eps = sb("eps", [P, 1])
        spare = sb("spare", [P, 1])
        gcol = sb("gcol", [P, 3, KC])
        col = sb("col", [P, 3, 2, KC])
        rt = sb("rt", [P, T])
        rs = sb("rs", [P, T])
        nmx = sb("nmx", [P, 2, 2, T])
        psm = sb("psm", [P, 2, 2, T])
        prc = sb("prc", [P, 2, 2, T])
        xe = sb("xe", [P, 2, KC, CAP])
        sil = reg_c[:, 1024:1280].rearrange("p (b f) -> p b f", b=2)
        he = reg_c[:, 1280:1536].rearrange("p (b f) -> p b f", b=2)
        heT = sb("heT", [P, 2, 2 * CAP])
        ye = sb("ye", [P, 2, D // 2])
        taken = [0]

        def scratch(shape):
            n = int(np.prod(shape[1:]))
            ap = ye[0:shape[0], :, :].rearrange("p b d -> p (b d)")[:, taken[0]:taken[0] + n]
            taken[0] += n
            assert taken[0] <= 2 * (D // 2)
            if len(shape) == 3:
                return ap.rearrange("p (a b) -> p a b", a=shape[1])
            return ap.rearrange("p (a b c) -> p a b c", a=shape[1], b=shape[2]) if len(shape) == 4 else ap

        lg = scratch([P, T, NG + E])
        gm = scratch([P, T, 1])
        gd = scratch([P, T, NG])
        gsum = scratch([P, T, 1])
        geq = scratch([P, T, NG])
        goh = scratch([P, T, NG])
        prod = scratch([P, T, NG, EPG])
        se = [scratch([P, T, EPG]) for i in range(2)]
        emx = [scratch([P, T, 1]) for i in range(2)]
        eeq = scratch([P, T, EPG])
        ecm = scratch([P, T, 1])
        eoh = [scratch([P, T, EPG]) for i in range(2)]
        ed = scratch([P, T, 1])
        eden = scratch([P, T, 1])
        wk = [scratch([P, T, 1]) for i in range(2)]
        msk = [scratch([P, T, E]) for i in range(2)]
        mask = scratch([P, T, E])
        cnt = scratch([P, E])
        endc = scratch([P, E])
        offc = scratch([P, E])
        posn = scratch([P, T, E])
        slot_of = [scratch([P, T, 1]) for i in range(2)]
        off_i = sb("off_i", [1, 2, E], I32)
        NC_ = SEQ // CAP - 1
        ov_ind = scratch([1, NC_, E])
        ov_n = scratch([1, E])
        ov_end = scratch([1, E])
        ov_rank = scratch([1, NC_, E])
        ov_start = scratch([1, NC_, E])
        ov_tmp = reg_c[0:1, 1536:1536 + NC_ * E].rearrange("p (q e) -> p q e", q=NC_)
        ov_last = scratch([1, E])
        ov_dump = reg_c[0:1, 1632:1632 + NC_ * E].rearrange("p (q e) -> p q e", q=NC_)
        ov_f = scratch([1, 2 * MAXOVF + SB])
        ov_i = sb("ov_i", [1, 2, 2 * MAXOVF + SB], I32)

        bank = [ctx.enter_context(nc.psum_tensor(f"bank{i}", [P, 512], F32)) for i in range(8)]

        def gate_w(s):
            return ring[:, s, 0:2048].rearrange("p (k f) -> p k f", k=KC)

        def up_w(s):
            return ring[:, s, 2048:4096].rearrange("p (k f) -> p k f", k=KC)

        def down_w(s):
            return ring[:, s, 4096:6144].rearrange("p (j d) -> p j d", j=2)

        def cols_w(s, n):
            return ring[:, s, 0:KC * n].rearrange("p (k n) -> p k n", k=KC)

        gate_d = exp_w_gate.rearrange("l e (p k) f -> l e p (k f)", k=KC)
        up_d = exp_w_up.rearrange("l e (p k) f -> l e p (k f)", k=KC)
        down_d = exp_w_down.rearrange("l e (j p) d -> l e p j d", p=P)
        ada_d = ada_w.rearrange("l (p k) n -> l p k n", k=KC)
        qkv_d = w_qkv.rearrange("l (p k) n -> l p k n", k=KC)
        wo_d = w_o.rearrange("l (m p) n -> l p m n", p=P)
        poolw_d = pool_w.rearrange("l g (c p) d -> l p (g c) d", p=P)
        x_d = x.rearrange("b (t p) d -> (b p) t d", p=P)
        out_d = out.rearrange("b (t p) d -> (b p) t d", p=P)

        def full_at(n):
            return 48 * (n // R + 1)

        def pieces(j):
            lo, hi = j * AC, (j + 1) * AC
            cut = -(-(lo + 1) // 512) * 512
            return [(lo, cut), (cut, hi)]

        def nth(L, w):
            return 2 * L + (w == "ffn")

        def flag(eng, L, s):
            n = 2 * MAXOVF + 1 + s
            return eng.value_load(ov_i[0:1, L, n:n + 1], min_val=0, max_val=1)

        by_tile = [(0, 0), (1, 0), (0, 1), (1, 1)]
        by_half = [(0, 0), (0, 1), (1, 0), (1, 1)]

        def sub_layer(L, w):
            if w == "fin":
                return S("x_moe", 1), by_tile
            if w == "mix":
                return S("x_moe", 0), by_tile
            return S("x_mixed", L), by_half if L else by_tile

        block = ctx.enter_context(nc.Block())

        @block.sync
        def _(sp):
            def split3(n, dst, src):
                if n >= R:
                    sp.wait_ge(S("ring_free", n % R), n // R)
                for a, b in ((0, 3), (3, 6), (6, 8)):
                    sp.dma_start(dst[:, a:b, :], src[:, a:b, :]).then_inc(S("ring_full", n % R), 16)

            def ada(a):
                L, j = divmod(a, 8)
                n = IT_ADA[a]
                split3(n, cols_w(n % R, AC), ada_d[L, :, :, j * AC:(j + 1) * AC])

            def expert(L, e, s, freed):
                if freed is not None:
                    sp.wait_ge(S("ring_free", s), freed)
                gsrc, usrc, dsrc = gate_d[L], up_d[L], down_d[L]
                sp.dma_start(ring[:, s, 0:2048], gsrc[bass.ds(e, 1), :, :].rearrange("a p n -> (a p) n"))\
                    .then_inc(S("ring_full", s), 16)
                sp.dma_start(ring[:, s, 2048:4096], usrc[bass.ds(e, 1), :, :].rearrange("a p n -> (a p) n"))\
                    .then_inc(S("ring_full", s), 16)
                sp.dma_start(down_w(s), dsrc[bass.ds(e, 1), :, :, :].rearrange("a p j d -> (a p) j d"))\
                    .then_inc(S("ring_full", s), 16)

            def experts(L, e0, e1):
                n0 = IT_EXP[L](e0)
                with sp.Fori(0, (e1 - e0) // R) as i:
                    for u in range(R):
                        n = n0 + u
                        expert(L, e0 + i * R + u, n % R, n // R + i)

            sp.dma_start(ccol[:, :], c.rearrange("b (p k) -> (b p) k", k=KC)).then_inc(S("c_loaded"), 16)
            ada(0)
            sp.dma_start(cst[:, :], misc).then_inc(S("misc_loaded"), 16)
            for L in range(2):
                sp.dma_start(rows[ROW_B[L]:ROW_B[L] + 6, :], ada_b[L].rearrange("(a d) -> a d", a=6))\
                    .then_inc(S("rows_loaded"), 16)
            sp.dma_start(rows[ROW_MIX:ROW_MIX + 1, :], norm_mix_g[0:1, :]).then_inc(S("rows_loaded"), 16)
            sp.dma_start(rows[ROW_PS:ROW_PS + 1, :], pool_scale).then_inc(S("rows_loaded"), 16)
            sp.dma_start(rows[ROW_FIN:ROW_FIN + 1, :], final_norm_g.rearrange("(a d) -> a d", a=1))\
                .then_inc(S("rows_loaded"), 16)
            ada(1)
            sp.dma_start(x_sb[:, :, :], x_d).then_inc(S("x_loaded"), 16)
            ada(2)
            sp.dma_start(band_sb, band.rearrange("p (t g q) -> p t g q", t=T, g=NG)).then_inc(S("band_loaded"), 16)
            ada(3)
            split3(IT_POOL, cols_w(IT_POOL % R, SEQ), poolw_d[0])
            sp.dma_start(gcol[:, 0:2, :], norm_ffn_g.rearrange("l (p k) -> p l k", k=KC)).then_inc(S("gcol_loaded"), 16)
            sp.dma_start(gcol[:, 2, :], norm_mix_g[1].rearrange("(p k) -> p k", k=KC)).then_inc(S("gcol_loaded"), 16)
            sp.dma_start(stage_g, router_group_w.rearrange("l (p k) n -> p l k n", k=KC)).then_inc(S("stage_loaded"), 16)
            sp.dma_start(stage_e, router_expert_w.rearrange("l (p k) n -> p l k n", k=KC)).then_inc(S("stage_loaded"), 16)
            for a in range(4, 11):
                ada(a)
            for e in range(R):
                n = IT_EXP[0](e)
                expert(0, e, n % R, n // R)
            ada(11)
            experts(0, R, E)
            adas, qkvs = iter(range(12, 16)), iter(enumerate(IT_QKV))
            for item in range(45, 53):
                if item in IT_ADA:
                    ada(next(adas))
                else:
                    j, n = next(qkvs)
                    split3(n, cols_w(n % R, AC), qkv_d[0, :, :, j * AC:(j + 1) * AC])
            for j, n in enumerate(IT_WO):
                split3(n, cols_w(n % R, 512), wo_d[0, :, :, j * 512:(j + 1) * 512])
            experts(1, 0, E)
            for t in range(T):
                for b in range(2):
                    sp.wait_ge(S("result_ready"), 2 * t + b + 1)
                    cols = slice(b * 512, b * 512 + 512)
                    sp.dma_start(out_d[:, t, cols], h_of[4][:, t, cols]).then_inc(S("stored"), 16)
            sp.wait_ge(S("stored"), 16 * 2 * T)

        @block.gpsimd
        def _(pool):
            nc.gpsimd.memset(ones[:, :], 1.0).then_inc(S("ones_ready"), 1)
            nc.gpsimd.memset(eps[:, :], EPS).then_inc(S("eps_ready"), 1)
            pool.wait_ge(S("stage_loaded"), 32)
            nc.gpsimd.tensor_copy(rw[:, :, :, 0:NG], stage_g).then_inc(S("rw_ready"), 1)
            nc.gpsimd.tensor_copy(rw[:, :, :, NG:NG + E], stage_e).then_inc(S("rw_ready"), 1)

            def pick_tokens(L, e, b):
                off = pool.value_load(off_i[0:1, L, bass.ds(e, 1)], min_val=0, max_val=NSLOT)
                nc.gpsimd.tensor_copy(xe[:, b, :, :], hS[:, :, bass.ds(off, CAP)]).then_inc(S("xe_ready", L), 1)

            for L in range(2):
                pool.wait_ge(S("off_ready"), L + 1)
                pool.wait_ge(S("hS_ready"), L * KC + KC)
                pool.wait_ge(S("hS_pad"), L + 1)
                pick_tokens(L, 0, 0)
                pick_tokens(L, 1, 1)
                with pool.Fori(1, E // 2) as i:
                    for b in range(2):
                        pool.wait_ge(S("gu_ready", L), i * 2 + (b - 1))
                        pick_tokens(L, i * 2 + b, b)
                pool.wait_ge(S("ovf_ready"), L + 1)
                pool.wait_ge(S("gu_ready", L), E)
                n_ovf = pool.value_load(ov_i[0:1, L, 2 * MAXOVF:2 * MAXOVF + 1], min_val=0, max_val=MAXOVF)
                with pool.If(n_ovf > 0):
                    with pool.Fori(0, n_ovf) as i:
                        off = pool.value_load(ov_i[0:1, L, bass.ds(i + MAXOVF, 1)], min_val=0, max_val=NSLOT)
                        pool.wait_ge(S("ovf_pe", L), i * 3 + 1)
                        nc.gpsimd.tensor_copy(xe[:, 0, :, :], hS[:, :, bass.ds(off, CAP)]).then_inc(S("ovf_xe", L), 1)

        @block.tensor
        def _(pe):
            def mm(o_, l_, r_, start, stop):
                return nc.tensor.matmul(o_, l_, r_, start=start, stop=stop)

            def row_bcast(o_, row, a, b, start=True):
                return mm(o_, ident[0:NROWS, row:row + 1].broadcast_to([NROWS, P]), rows[:, a:b], start, True)

            def part(a):
                n = IT_ADA[a]
                w = cols_w(n % R, AC)
                if a == 0:
                    pe.wait_ge(S("cact_ready"), 1)
                pe.wait_ge(S("ring_full", n % R), full_at(n))
                if a:
                    pe.wait_ge(S("acc_ready"), 2 * a)
                else:
                    pe.wait_ge(S("misc_loaded"), 16)
                    pe.wait_ge(S("rows_loaded"), 16 * 5)
                for b, (lo, hi) in enumerate(((0, 512), (512, AC))):
                    for kk in range(2):
                        for g in range(4):
                            k = 4 * kk + g
                            mm(bank[4 + b][32 * g:32 * g + 32, 0:hi - lo],
                               cact[:, k:k + 1].broadcast_to([P, 32]), w[:, k, lo:hi], kk == 0, False)
                    q = (hi - lo) // 4
                    for g in range(4):
                        row, col0 = divmod(a % 8 * AC + lo + g * q, D)
                        row += ROW_B[a // 8]
                        last = mm(bank[4 + b][32 * g:32 * g + 32, g * q:(g + 1) * q],
                                  ident[0:NROWS, row:row + 1].broadcast_to([NROWS, 32]), rows[:, col0:col0 + q],
                                  False, True)
                    last.then_inc(S("part_full"), 1)

            def bcast(a):
                L, j = divmod(a, 8)
                if a == 0:
                    pe.wait_ge(S("ones_ready"), 1)
                if a >= 1:
                    pe.wait_ge(S("mod_written"), 2 * a)
                pe.wait_ge(S("acc_ready"), 2 * (a + 1))
                c0 = j * AC
                for b, (lo, hi) in enumerate(pieces(j)):
                    row, col = divmod(lo, D)
                    dst = bank[6 + b][:, 0:hi - lo]
                    if a < ADA_PE:
                        last = mm(dst, quarter, acc[:, a % 2, lo - c0:hi - c0], True, True)
                    else:
                        mm(dst, ones[:, :], acc[:, a % 2, lo - c0:hi - c0], True, False)
                        last = row_bcast(dst, ROW_B[L] + row, col, col + hi - lo, start=False)
                    last.then_inc(S("bcast_ready"), 1)

            def ada(a):
                part(a)
                bcast(a)

            def gain(row, b0, name):
                for b in range(2):
                    row_bcast(bank[b0 + b][:, :], row, b * 512, b * 512 + 512).then_inc(S(name), 1)

            def column(jv, dst):
                vec = mod[0:1, jv * D:(jv + 1) * D].rearrange("o (p k) -> o k p", k=KC)
                for k in range(KC):
                    mm(dst[:, k:k + 1], vec[:, k, :], ones[0:1, 0:1], True, True).then_inc(S("cols_full"), 1)

            def columns(ja, jb, dst):
                column(ja, dst[:, 0:KC])
                column(jb, dst[:, KC:2 * KC])

            def transposes(L, w):
                i = nth(L, w)
                xr = h_of[i].rearrange("p t (q k) -> p t k q", k=KC)
                for t in range(T):
                    pe.wait_ge(S("xr_ready"), (nth(L, w) - 1) * T + t + 1)
                    for k in range(KC):
                        last = nc.tensor.transpose(bank[hT_bank[i] + 2 * t + k // 4][:, k % 4 * P:(k % 4 + 1) * P],
                                                   xr[:, t, k, :], ident)
                        if k % 4 == 3:
                            last.then_inc(S("hT_full"), 1)

            def hT_written(L, w, t):
                for eng in ("act", "dve"):
                    pe.wait_ge(S("hT_" + eng), (nth(L, w) - 1) * T * KC // 2 + (t + 1) * KC // 2)

            def route(L):
                if L == 0:
                    pe.wait_ge(S("rw_ready"), 2)
                for t in range(T):
                    hT_written(L, "ffn", t)
                    for k in range(KC):
                        last = mm(bank[0][:, t * 36:t * 36 + 36], hT[:, k, t * P:(t + 1) * P], rw[:, L, k, :],
                                  k == 0, k == KC - 1)
                last.then_inc(S("logits"), 1)
                if L == 0:
                    part(7)
                    part(8)
                    bcast(7)
                pe.wait_ge(S("mask_ready"), L + 1)
                for t in range(T):
                    mm(bank[1][:, 0:E], ones[:, :], mask[:, t, :], t == 0, t == T - 1)
                mm(bank[1][:, E:2 * E], tri, mask[:, 0, :], True, True)
                mm(bank[1][:, 2 * E:3 * E], ones[:, :], mask[:, 0, :], True, False)
                mm(bank[1][:, 2 * E:3 * E], tri, mask[:, 1, :], False, True).then_inc(S("counts"), 1)

            def gather(L):
                pe.wait_ge(S("pick_ready"), L * T + T)
                for k in range(KC):
                    if k >= 4:
                        pe.wait_ge(S("hS_ready"), L * KC + k - 3)
                    for t in range(T):
                        last = mm(bank[k % 4][:, :], h_str[:, t, k, :], pick[:, t, :], t == 0, t == T - 1)
                    last.then_inc(S("gathered"), 1)
                pe.wait_ge(S("pickw_ready"), L * T + T)
                for b in range(2):
                    for s in range(2):
                        for t in range(T):
                            last = nc.tensor.transpose(bank[6 + b][:, s * SEQ + t * P:s * SEQ + (t + 1) * P],
                                                       pickw[:, t, (2 * b + s) * P:(2 * b + s + 1) * P], ident)
                    last.then_inc(S("pwT_full"), 1)

            def hidden(dst, w, b):
                for k in range(KC):
                    for j in range(2):
                        last = mm(dst[j * CAP:(j + 1) * CAP, :], xe[:, b, k, :], w(k, j), k == 0, k == KC - 1)
                return last

            def turn_he(dst, b):
                return nc.tensor.transpose(dst[:, 2 * P:3 * P], he[:, b, :], ident)

            def down(dst, wd, b):
                for j in range(2):
                    for half in range(2):
                        last = mm(dst[half * CAP:(half + 1) * CAP, :], heT[:, b, j * CAP:(j + 1) * CAP],
                                  wd[:, j, :].rearrange("p (c h q) -> p h c q", c=4, h=2)[:, half, :, :],
                                  j == 0, j == 1)
                return last

            def turn_ye(dst, b):
                for cq in range(4):
                    last = nc.tensor.transpose(dst[:, cq * P:(cq + 1) * P], ye[:, b, cq * P:(cq + 1) * P], ident)
                return last

            def expert(L, e, s, fill, b, first=False):
                gu = ring[:, s, 0:4096].rearrange("p (g k j f) -> p k j g f", g=2, k=KC, j=2)
                pe.wait_ge(S("xe_ready", L), e + 1)
                pe.wait_ge(S("ring_full", s), fill)
                pe.wait_ge(S("heT_ready", L), e + 1)
                hidden(bank[b][:, 0:F], lambda k, j: gu[:, k, j, :, :], b).then_inc(S("gu_ready", L), 1)
                if not first:
                    turn_last(L, e, 1 - b)
                pe.wait_ge(S("he_ready", L), e + 1)
                turn_he(bank[b], b).then_inc(S("he_turned", L), 1)
                pe.wait_ge(S("heT_ready", L), e + 3)
                pe.wait_ge(S("dn_free", L), e + 1)
                down(bank[2 + b], down_w(s), b).then_inc(S("dn_ready", L), 1)

            def turn_last(L, e, b):
                pe.wait_ge(S("ye_ready", L), e)
                turn_ye(bank[2 + b], b).then_inc(S("ye_turned", L), 1)

            def experts(L, e0, e1):
                n0 = IT_EXP[L](e0)
                with pe.Fori(0, (e1 - e0) // R) as i:
                    for u in range(R):
                        n = n0 + u
                        expert(L, i * R + (e0 + u), n % R, i * 48 + full_at(n), u % 2)

            def expert_at(L, e):
                n = IT_EXP[L](e)
                expert(L, e, n % R, full_at(n), e % 2, first=e == 0)

            def overflow(L):
                pe.wait_ge(S("ovf_ready"), L + 1)
                n_ovf = pe.value_load(ov_i[0:1, L, 2 * MAXOVF:2 * MAXOVF + 1], min_val=0, max_val=MAXOVF)
                pe.sem_inc(S("ovf_pe", L), 1)
                w = reg_h[:, :].rearrange("p (k j f) -> p k j f", k=KC, j=2)
                wd = reg_h[:, :].rearrange("p (j d) -> p j d", j=2)
                with pe.If(n_ovf > 0):
                    with pe.Fori(0, n_ovf) as i:
                        pe.wait_ge(S("ovf_xe", L), i + 1)
                        for g in range(2):
                            pe.wait_ge(S("ovf_w", L), i * 48 + 16 * (g + 1))
                            hidden(bank[0][:, g * P:(g + 1) * P], lambda k, j: w[:, k, j, :], 0)\
                                .then_inc(S("ovf_pe", L), 1)
                        pe.wait_ge(S("ovf_he", L), i + 1)
                        turn_he(bank[0], 0).then_inc(S("ovf_he_turned", L), 1)
                        pe.wait_ge(S("ovf_w", L), i * 48 + 48)
                        pe.wait_ge(S("ovf_heT", L), i + 1)
                        down(bank[2], wd, 0).then_inc(S("ovf_pe", L), 1)
                        pe.wait_ge(S("ovf_ye", L), i + 1)
                        turn_ye(bank[2], 0).then_inc(S("ovf_turned", L), 1)
                    pe.wait_ge(S("ovf_y", L), n_ovf)

            def combine(L, s):
                for half in range(2):
                    for mq in range(4):
                        last = nc.tensor.transpose(bank[half][:, mq * P:(mq + 1) * P],
                                                   yT[:, half * 4 + mq, s * P:(s + 1) * P], ident)
                    last.then_inc(S("yT_turned", L), 1)
                pe.wait_ge(S("yS_act", L), s + 1)
                pe.wait_ge(S("yS_dve", L), s + 1)
                for half, t in by_tile:
                    last = mm(bank[4 + half + 2 * t][:, :], pwT[:, s, t * P:(t + 1) * P],
                              yS[s][:, half * 512:half * 512 + 512], s == 0, s == SB - 1)
                    if s == SB - 1:
                        last.then_inc(S("moe_out", L), 1)

            def later_experts(L):
                experts(L, R, STAGES[0])
                pe.wait_ge(S("pwT_ready"), 2 * (L + 1))
                pe.wait_ge(S("cols_ready") if L == 0 else S("gain_kept"), 2)
                for s, e in enumerate(STAGES):
                    expert_at(L, e)
                    pe.wait_ge(S("dn_free", L), e + 2)
                    with pe.If(flag(pe, L, s) > 0):
                        combine(L, s)
                    for u in range(1, R):
                        expert_at(L, e + u)
                all_early = flag(pe, L, SB - 2)
                turn_last(L, E, 1)
                pe.wait_ge(S("dn_free", L), E + 2)
                with pe.If(all_early < 1):
                    overflow(L)
                    for s in range(SB - 1):
                        with pe.If(flag(pe, L, s) < 1):
                            combine(L, s)
                combine(L, SB - 1)

            for a in range(3):
                ada(a)
            pe.wait_ge(S("mod_written"), 2 * 3)
            gain(ROW_MIX, 6, "gain_mix")
            part(3)
            pe.wait_ge(S("A_ready"), 2)
            bcast(3)
            pe.wait_ge(S("h_ready"), T)
            pe.wait_ge(S("band_loaded"), 16)
            for m in range(KC):
                for t in range(T):
                    last = mm(bank[m // 2][:, (m % 2) * SEQ:(m % 2 + 1) * SEQ], h[:, t, m * P:(m + 1) * P],
                              band_sb[:, t, m // 2, :], t == 0, t == T - 1)
                if m % 2:
                    last.then_inc(S("pT_full"), 1)
            pe.wait_ge(S("mod_written"), 2 * 4)
            gain(ROW_PS, 6, "gain_ps")
            pe.wait_ge(S("pT_ready"), 4)
            pe.wait_ge(S("ring_full", IT_POOL % R), full_at(IT_POOL))
            pw = cols_w(IT_POOL % R, SEQ)
            for half, t in by_tile:
                for gg in range(2):
                    for cc in range(2):
                        m = (2 * half + gg) * 2 + cc
                        last = mm(bank[half + 2 * t][:, gg * SEQ:(gg + 1) * SEQ], pT[:, m, t * P:(t + 1) * P],
                                  pw[:, m, :], cc == 0, cc == 1)
                last.then_inc(S("mix_out", 0), 1)
            pe.wait_ge(S("mix_out", 0), 2 * T)
            pe.sem_inc(S("ring_free", IT_POOL % R), 1)
            part(4)
            transposes(0, "ffn")
            pe.wait_ge(S("ps_used"), 2)
            part(5)
            bcast(4)
            part(6)
            bcast(5)
            pe.wait_ge(S("acc_ready"), 2 * 7)
            pe.wait_ge(S("mod_written"), 2 * 6)
            column(3, bank[4][:, KC:2 * KC])
            bcast(6)
            pe.wait_ge(S("mod_written"), 2 * 7)
            column(4, bank[4][:, 0:KC])
            route(0)
            part(9)
            bcast(8)
            part(10)
            pe.wait_ge(S("mod_written"), 2 * 9)
            gather(0)
            pe.wait_ge(S("pwT_ready"), 2)
            bcast(9)
            bcast(10)
            for e in range(R):
                expert_at(0, e)
            ada(11)
            pe.wait_ge(S("mod_written"), 2 * 12)
            columns(1, 0, bank[6])
            later_experts(0)

            transposes(1, "mix")
            hT_written(1, "mix", 1)
            u = 0
            for j, n in enumerate(IT_QKV):
                pe.wait_ge(S("ring_full", n % R), full_at(n))
                w = cols_w(n % R, AC)
                for col in range(j * AC, (j + 1) * AC, P):
                    m = col // P
                    if m >= 16 and m % 2:
                        continue
                    for t in range(1 if m < 16 else T):
                        if u >= 4:
                            pe.wait_ge(S("qkv_read"), u - 3)
                        for k in range(KC):
                            c0 = col - j * AC
                            if m < 16:
                                last = mm(bank[u % 4][:, 0:SEQ], w[:, k, c0:c0 + P], hT[:, k, :], k == 0, k == KC - 1)
                            else:
                                last = mm(bank[u % 4][:, 0:SEQ], hT[:, k, t * P:(t + 1) * P], w[:, k, c0:c0 + 256],
                                          k == 0, k == KC - 1)
                        last.then_inc(S("qkv_full"), 1)
                        u += 1
                pe.wait_ge(S("qkv_full"), u)
                pe.sem_inc(S("ring_free", n % R), 1)
                if j >= 1:
                    bcast(12 + j - 1)
            pe.wait_ge(S("qkv_read"), u)
            bcast(15)
            pe.wait_ge(S("mod_written"), 2 * 16)

            def scores(m):
                for t in range(T):
                    for a in range(2):
                        rows_a = slice(a * DH, (a + 1) * DH)
                        last = mm(bank[1 + 2 * (m % 2) + a][:, t * P:t * P + (t + 1) * P],
                                  qT[rows_a, m, t * P:(t + 1) * P], kT[rows_a, m, 0:(t + 1) * P], True, True)
                        if t == T - 1:
                            last.then_inc(S("s_full"), 1)

            def turn(m):
                pe.wait_ge(S("prT_ready"), 2 * m)
                for a in range(2):
                    pe.wait_ge(S("p_ready"), 4 * m + 2 * a + 2)
                    for s in range(3):
                        last = nc.tensor.transpose(bank[5 + a][:, s * P:(s + 1) * P],
                                                   sc[m % 2][a][:, s * P:(s + 1) * P], ident)
                    last.then_inc(S("pT_turned"), 1)

            def weigh(m):
                pe.wait_ge(S("prT_ready"), 2 * m + 2)
                if m >= 2:
                    pe.wait_ge(S("o_read"), m - 1)
                bk = bank[7 * (m % 2)]
                for t in range(T):
                    for a in range(2):
                        last = mm(bk[a * DH:(a + 1) * DH, t * P:SEQ], v[:, t, m * P + a * DH:m * P + (a + 1) * DH],
                                  prT[m % 2][a][:, t * SEQ:t * P + SEQ], t == 0, t == T - 1)
                last.then_inc(S("pv_done"), 1)

            scores(0)
            scores(1)
            for m in range(NH // 2):
                turn(m)
                if m + 2 < NH // 2:
                    pe.wait_ge(S("s_read"), 2 * m + 2)
                    if m == 1:
                        columns(4, 3, bank[3][:, 3 * P:4 * P])
                    scores(m + 2)
                if m:
                    weigh(m - 1)
            weigh(NH // 2 - 1)
            pe.wait_ge(S("o_read"), NH // 2)
            for j, n in enumerate(IT_WO):
                pe.wait_ge(S("ring_full", n % R), full_at(n))
                w = cols_w(n % R, 512)
                for t in range(T):
                    for m in range(KC):
                        last = mm(bank[j + 2 * t][:, :], oT[:, m, t * P:(t + 1) * P], w[:, m, :], m == 0, m == KC - 1)
                    last.then_inc(S("mix_out", 1), 1)
                pe.wait_ge(S("mix_out", 1), T * (j + 1))
                pe.sem_inc(S("ring_free", n % R), 1)
            transposes(1, "ffn")
            route(1)
            gather(1)
            for e in range(R):
                expert_at(1, e)
            gain(ROW_FIN, 4, "gain_fin")
            later_experts(1)

        @block.scalar
        def _(act):
            def copy(o_, i_):
                return nc.scalar.activation(o_, i_, ACT.Identity)

            def mean_square_root(i, t):
                nc.scalar.activation(h_of[i][:, t, :], x_sb[:, t, :], ACT.Square, accum_out=ss[:, t:t + 1])\
                    .then_inc(S("ss_ready"), 1)
                act.wait_ge(S("ss_ready"), i * T + t + 1)
                nc.scalar.activation(rt[:, t:t + 1], ss[:, t:t + 1], ACT.Sqrt, bias=eps[:, :], scale=1.0 / D)\
                    .then_inc(S("rt_ready"), 1)

            def rms(L, w):
                pieces_done, order = sub_layer(L, w)
                i = nth(L, w)
                for t in range(T):
                    act.wait_ge(pieces_done, order.index((1, t)) + 1)
                    mean_square_root(i, t)
                    if w != "fin":
                        act.wait_ge(S("rs_ready"), i * T + t + 1)
                        nc.scalar.activation(h_of[i][:, t, :], x_sb[:, t, :], ACT.Identity, scale=rs[:, t:t + 1])\
                            .then_inc(S("xr_ready"), 1)
                    if L == 1:
                        evac_hT(L, w, t)

            def take_part(a):
                for b, (lo, hi) in enumerate(((0, 512), (512, AC))):
                    act.wait_ge(S("part_full"), 2 * a + b + 1)
                    if b:
                        act.sem_inc(S("ring_free", IT_ADA[a] % R), 1)
                    copy(acc[:, a % 2, lo:hi], bank[4 + b][:, 0:hi - lo]).then_inc(S("acc_ready"), 1)

            def ada(a):
                take_part(a)
                write_mod(a)

            def write_mod(a):
                for b, (lo, hi) in enumerate(pieces(a % 8)):
                    act.wait_ge(S("bcast_ready"), 2 * a + b + 1)
                    copy(mod[:, lo:hi], bank[6 + b][:, 0:hi - lo]).then_inc(S("mod_written"), 1)

            def scaled(o_, i_, i, k):
                return nc.scalar.activation(o_, i_, ACT.Identity, scale=col[:, i, 0, k:k + 1], bias=col[:, i, 1, k:k + 1])

            def evac_hT(L, w, t):
                i = nth(L, w) - 1
                act.wait_ge(S("cols_ready"), i + 1)
                act.wait_ge(S("hT_full"), (i * T + t) * 2 + 1)
                for k in range(KC // 2):
                    scaled(hT[:, k, t * P:(t + 1) * P], bank[hT_bank[i + 1] + 2 * t][:, k * P:(k + 1) * P], i, k)\
                        .then_inc(S("hT_act"), 1)

            def route(L):
                act.wait_ge(S("gd_ready"), L + 1)
                nc.scalar.activation(gd[:, :, :], gd[:, :, :], ACT.Exp).then_inc(S("gexp"), 1)
                act.wait_ge(S("ed_ready"), L + 1)
                nc.scalar.activation(ed[:, :, :], ed[:, :, :], ACT.Exp).then_inc(S("gexp"), 1)

            def evac_gather(L):
                for k in range(KC):
                    act.wait_ge(S("gathered"), L * KC + k + 1)
                    last = scaled(hS[:, k, 0:NSLOT], bank[k % 4][:, :], nth(L, "ffn") - 1, k)
                    last.then_inc(S("hS_ready"), 1)
                for b in range(2):
                    act.wait_ge(S("pwT_full"), L * 2 + b + 1)
                    copy(pwT[:, 2 * b:2 * b + 2, :], bank[6 + b][:, :].rearrange("p (s q) -> p s q", s=2))\
                        .then_inc(S("pwT_ready"), 1)
                act.wait_ge(S("hS_ready"), L * KC + KC)
                act.sem_inc(S("heT_ready", L), 2)
                act.sem_inc(S("dn_free", L), 2)
                if L:
                    load_table(ACT.Silu)

            def silu(L, e, b):
                act.wait_ge(S("gu_ready", L), e + 1)
                nc.scalar.activation(sil[:, b, :], bank[b][:, 0:P], ACT.Silu).then_inc(S("sil_ready", L), 1)

            def yT_at(off):
                return yT[:, :, bass.ds(off, CAP)]

            def from_turned(b):
                return b[:, :].rearrange("p (m s) -> p m s", m=KC)

            def load_table(func):
                nc.scalar.activation(spare[:, :], eps[:, :], func)

            def put_y(L, e, b):
                off = act.value_load(off_i[0:1, L, bass.ds(e, 1)], min_val=0, max_val=NSLOT)
                act.wait_ge(S("ye_turned", L), e + 1)
                act.wait_ge(S("dn_free", L), e + 2)
                copy(yT_at(off), from_turned(bank[2 + b])).then_inc(S("dn_free", L), 1)

            def experts(L, e0, e1):
                with act.Fori(0, (e1 - e0) // R) as i:
                    for u in range(R):
                        silu(L, i * R + (e0 + u), u % 2)
                        put_y(L, i * R + (e0 + u - 1), 1 - u % 2)

            def expert_at(L, e):
                silu(L, e, e % 2)
                if e:
                    put_y(L, e - 1, 1 - e % 2)

            def overflow(L):
                act.wait_ge(S("dn_free", L), E + 2)
                n_ovf = act.value_load(ov_i[0:1, L, 2 * MAXOVF:2 * MAXOVF + 1], min_val=0, max_val=MAXOVF)
                with act.If(n_ovf > 0):
                    with act.Fori(0, n_ovf) as i:
                        e = act.value_load(ov_i[0:1, L, bass.ds(i, 1)], min_val=0, max_val=E - 1)
                        off = act.value_load(ov_i[0:1, L, bass.ds(i + MAXOVF, 1)], min_val=0, max_val=NSLOT)
                        act.wait_ge(S("ovf_pe", L), i * 3 + 1)
                        act.dma_start(reg_h[:, :], gate_d[L][bass.ds(e, 1), :, :].rearrange("a p n -> (a p) n"))\
                            .then_inc(S("ovf_w", L), 16)
                        act.wait_ge(S("ovf_pe", L), i * 3 + 2)
                        act.dma_start(reg_h[:, :], up_d[L][bass.ds(e, 1), :, :].rearrange("a p n -> (a p) n"))\
                            .then_inc(S("ovf_w", L), 16)
                        act.wait_ge(S("ovf_pe", L), i * 3 + 3)
                        act.dma_start(reg_h[:, :].rearrange("p (j d) -> p j d", j=2),
                                      down_d[L][bass.ds(e, 1), :, :, :].rearrange("a p j d -> (a p) j d"))\
                            .then_inc(S("ovf_w", L), 16)
                        nc.scalar.activation(sil[:, 0, :], bank[0][:, 0:P], ACT.Silu).then_inc(S("ovf_sil", L), 1)
                        act.wait_ge(S("ovf_turned", L), i + 1)
                        copy(yT_at(off), from_turned(bank[2])).then_inc(S("ovf_y", L), 1)
                        act.wait_ge(S("ovf_y", L), i + 1)

            def evac_yT(L, s):
                act.wait_ge(S("yT_turned", L), 2 * s + 1)
                copy(yS[s][:, 0:512], bank[0][:, :]).then_inc(S("yS_act", L), 1)

            def later_experts(L):
                experts(L, R, STAGES[0])
                for s, e in enumerate(STAGES):
                    expert_at(L, e)
                    with act.If(flag(act, L, s) > 0):
                        evac_yT(L, s)
                    for u in range(1, R):
                        expert_at(L, e + u)
                all_early = flag(act, L, SB - 2)
                put_y(L, E - 1, 1)
                with act.If(all_early < 1):
                    overflow(L)
                    for s in range(SB - 1):
                        with act.If(flag(act, L, s) < 1):
                            evac_yT(L, s)
                evac_yT(L, SB - 1)
                load_table(ACT.Sqrt)

            def keep_gain():
                for b in range(2):
                    act.wait_ge(S("gain_fin"), b + 1)
                    copy(mod[:, b * 512:(b + 1) * 512], bank[4 + b][:, :]).then_inc(S("gain_kept"), 1)

            act.wait_ge(S("c_loaded"), 16)
            nc.scalar.activation(cact[:, :], ccol[:, :], ACT.Silu).then_inc(S("cact_ready"), 1)
            ada(0)
            ada(1)
            act.wait_ge(S("x_loaded"), 16)
            act.wait_ge(S("eps_ready"), 1)
            for t in range(T):
                mean_square_root(0, t)
            ada(2)
            ada(3)
            for b in range(4):
                act.wait_ge(S("pT_full"), b + 1)
                copy(pT[:, 2 * b:2 * b + 2, :], bank[b][:, :].rearrange("p (m q) -> p m q", m=2))\
                    .then_inc(S("pT_ready"), 1)
            rms(0, "ffn")
            take_part(4)
            take_part(5)
            write_mod(4)
            take_part(6)
            write_mod(5)
            write_mod(6)
            evac_hT(0, "ffn", 0)
            evac_hT(0, "ffn", 1)
            take_part(7)
            take_part(8)
            write_mod(7)
            route(0)
            take_part(9)
            write_mod(8)
            take_part(10)
            evac_gather(0)
            write_mod(9)
            write_mod(10)
            for e in range(R):
                expert_at(0, e)
            ada(11)
            later_experts(0)
            rms(1, "mix")
            u = 0
            for j in range(4):
                for m in range(6 * j, 6 * j + 6):
                    if m >= 16 and m % 2:
                        continue
                    for t in range(1 if m < 16 else T):
                        act.wait_ge(S("qkv_full"), u + 1)
                        src = bank[u % 4][:, 0:SEQ]
                        if m < 8:
                            last = nc.scalar.activation(qT[:, m, :], src, ACT.Identity, scale=DH ** -0.5)
                        elif m < 16:
                            last = copy(kT[:, m - 8, :], src)
                        else:
                            last = copy(v[:, t, (m - 16) * P:(m - 14) * P], src)
                        last.then_inc(S("qkv_read"), 1)
                        u += 1
                if j >= 1:
                    write_mod(12 + j - 1)

            write_mod(15)
            load_table(ACT.Exp)

            def exps(m):
                for a in range(2):
                    p = sc[m % 2][a]
                    act.wait_ge(S("mx_ready"), 4 * m + 2 * a + 2)
                    for t in range(T):
                        cols = slice(t * P, t * P + (t + 1) * P)
                        nc.scalar.activation(p[:, cols], p[:, cols], ACT.Exp, bias=nmx[:, m % 2, a, t:t + 1],
                                             accum_out=psm[:, m % 2, a, t:t + 1]).then_inc(S("exp_done"), 1)

            def evac_prT(m):
                if m >= 2:
                    act.wait_ge(S("pv_done"), m - 1)
                for a in range(2):
                    act.wait_ge(S("pT_turned"), 2 * m + a + 1)
                    copy(prT[m % 2][a], bank[5 + a][:, 0:3 * P]).then_inc(S("prT_ready"), 1)

            def evac_o(m):
                act.wait_ge(S("pv_done"), m + 1)
                copy(oT[:, m, :], bank[7 * (m % 2)][:, 0:SEQ]).then_inc(S("o_read"), 1)

            exps(0)
            exps(1)
            for m in range(NH // 2):
                evac_prT(m)
                if m + 2 < NH // 2:
                    exps(m + 2)
                if m:
                    evac_o(m - 1)
            evac_o(NH // 2 - 1)
            load_table(ACT.Sqrt)
            rms(1, "ffn")
            route(1)
            evac_gather(1)
            for e in range(R):
                expert_at(1, e)
            keep_gain()
            later_experts(1)
            rms(2, "fin")

        @block.vector
        def _(dve):
            steps = [0]

            def then(ins):
                steps[0] += 1
                ins.then_inc(S("dve_step"), 1)
                dve.wait_ge(S("dve_step"), steps[0])

            def tt(o_, a_, b_, op):
                return nc.vector.tensor_tensor(o_, a_, b_, op)

            def stt(o_, a_, s_, b_, op0, op1):
                return nc.vector.scalar_tensor_tensor(o_, a_, s_, b_, op0, op1)

            def ada(a):
                n = IT_ADA[a]
                w = cols_w(n % R, AC)
                dve.wait_ge(S("ring_full", n % R), full_at(n))
                if a >= 2:
                    dve.wait_ge(S("bcast_ready"), 2 * (a - 1))
                for k in range(KC):
                    for hf in range(2):
                        cols = slice(hf * AC // 2, (hf + 1) * AC // 2)
                        dst = acc[:, a % 2, cols]
                        if k == 0:
                            ins = nc.vector.tensor_scalar(dst, w[:, k, cols], cact[:, k:k + 1], None, ALU.mult)
                        else:
                            dve.wait_ge(S("acc_step"), 2 * (KC - 1) * (a - ADA_PE) + 2 * (k - 1) + hf + 1)
                            ins = stt(dst, w[:, k, cols], cact[:, k:k + 1], dst, ALU.mult, ALU.add)
                        if k < KC - 1:
                            ins.then_inc(S("acc_step"), 1)
                        else:
                            ins.then_inc(S("acc_ready"), 1)
                dve.wait_ge(S("acc_ready"), 2 * (a + 1))
                dve.sem_inc(S("ring_free", n % R), 1)

            def reciprocals(i, t):
                dve.wait_ge(S("rt_ready"), i * T + t + 1)
                nc.vector.reciprocal(rs[:, t:t + 1], rt[:, t:t + 1]).then_inc(S("rs_ready"), 1)

            def norm_mix():
                dve.wait_ge(S("mod_written"), 2 * 3)
                for b in range(2):
                    dve.wait_ge(S("gain_mix"), b + 1)
                    cols = slice(D + b * 512, D + b * 512 + 512)
                    stt(mod[:, cols], mod[:, cols], 1.0, bank[6 + b][:, :], ALU.add, ALU.mult)\
                        .then_inc(S("A_ready"), 1)
                dve.wait_ge(S("A_ready"), 2)
                dve.wait_ge(S("rs_ready"), T)
                for t in range(T):
                    stt(h[:, t, :], x_sb[:, t, :], rs[:, t:t + 1], mod[:, D:2 * D], ALU.mult, ALU.mult)\
                        .then_inc(S("h_scaled"), 1)
                for t in range(T):
                    dve.wait_ge(S("h_scaled"), t + 1)
                    tt(h[:, t, :], h[:, t, :], mod[:, 0:D], ALU.add).then_inc(S("h_ready"), 1)

            def columns(i, src):
                if i == 0:
                    dve.wait_ge(S("gcol_loaded"), 32)
                dve.wait_ge(S("cols_full"), 2 * KC * (i + 1))
                then(stt(col[:, i, 0, :], src[:, 0:KC], 1.0, gcol[:, (0, 2, 1)[i], :], ALU.add, ALU.mult))
                nc.vector.tensor_copy(col[:, i, 1, :], src[:, KC:2 * KC]).then_inc(S("cols_ready"), 1)
                dve.wait_ge(S("cols_ready"), i + 1)

            def add_to_x(ready, sub, jg, tmp, b0, after):
                done, order = sub
                for i, (half, t) in enumerate(order):
                    cols = slice(half * 512, half * 512 + 512)
                    dve.wait_ge(ready, i + 1)
                    then(tt(tmp, bank[b0 + half + 2 * t][:, :], mod[:, jg * D + half * 512:jg * D + half * 512 + 512], ALU.mult))
                    tt(x_sb[:, t, cols], x_sb[:, t, cols], tmp, ALU.add).then_inc(done, 1)
                    dve.wait_ge(done, i + 1)
                    if half == 1 and order is by_half:
                        after(t)
                if order is by_tile:
                    for t in range(T):
                        after(t)

            def evac_hT(L, w, t):
                i = nth(L, w) - 1
                dve.wait_ge(S("hT_full"), (i * T + t) * 2 + 2)
                for k in range(KC // 2, KC):
                    nc.vector.tensor_scalar(hT[:, k, t * P:(t + 1) * P],
                                            bank[hT_bank[i + 1] + 2 * t + 1][:, k % 4 * P:(k % 4 + 1) * P],
                                            col[:, i, 0, k:k + 1], col[:, i, 1, k:k + 1], ALU.mult, ALU.add)\
                        .then_inc(S("hT_dve"), 1)

            def norm_step(L, w):
                def after(t):
                    reciprocals(nth(L, w), t)
                    evac_hT(L, w, t)
                return after

            def wide(ap, n):
                return ap.broadcast_to([P, T, n])

            def first_max(val, mx, n, oh, eq, cm):
                then(nc.vector.tensor_reduce(mx, val, AX, ALU.max))
                then(tt(eq, val, wide(mx, n), ALU.is_equal))
                then(tt(eq, eq, first8[:, EPG - n:EPG].unsqueeze(1).broadcast_to([P, T, n]), ALU.mult))
                then(nc.vector.tensor_reduce(cm, eq, AX, ALU.max))
                then(tt(oh, eq, wide(cm, n), ALU.is_equal))

            def route(L):
                dve.wait_ge(S("logits"), L + 1)
                then(nc.vector.tensor_copy(lg[:, :, :], bank[0][:, 0:T * 36].rearrange("p (t n) -> p t n", t=T)))
                first_max(lg[:, :, 0:NG], gm[:, :, :], NG, goh[:, :, :], geq[:, :, :], ecm[:, :, :])
                tt(gd[:, :, :], lg[:, :, 0:NG], wide(gm[:, :, :], NG), ALU.subtract).then_inc(S("gd_ready"), 1)
                el = lg[:, :, NG:NG + E].rearrange("p t (g j) -> p t g j", g=NG)
                for t in range(T):
                    last = tt(prod[:, t, :, :], el[:, t, :, :],
                              goh[:, t, :].unsqueeze(2).broadcast_to([P, NG, EPG]), ALU.mult)
                then(last)
                then(nc.vector.tensor_reduce(se[0][:, :, :], prod[:, :, :, :].rearrange("p t g j -> p t j g"), AX, ALU.add))
                first_max(se[0][:, :, :], emx[0][:, :, :], EPG, eoh[0][:, :, :], eeq[:, :, :], ecm[:, :, :])
                then(stt(se[1][:, :, :], eoh[0][:, :, :], -BIG, se[0][:, :, :], ALU.mult, ALU.add))
                first_max(se[1][:, :, :], emx[1][:, :, :], EPG, eoh[1][:, :, :], eeq[:, :, :], ecm[:, :, :])
                tt(ed[:, :, :], emx[1][:, :, :], emx[0][:, :, :], ALU.subtract).then_inc(S("ed_ready"), 1)
                for i in range(2):
                    for t in range(T):
                        last = tt(msk[i][:, t, :].rearrange("p (g j) -> p g j", g=NG),
                                  goh[:, t, :].unsqueeze(2).broadcast_to([P, NG, EPG]),
                                  eoh[i][:, t, :].unsqueeze(1).broadcast_to([P, NG, EPG]), ALU.mult)
                then(last)
                tt(mask[:, :, :], msk[0][:, :, :], msk[1][:, :, :], ALU.add).then_inc(S("mask_ready"), 1)
                dve.wait_ge(S("gexp"), L * 2 + 2)
                then(nc.vector.tensor_reduce(gsum[:, :, :], gd[:, :, :], AX, ALU.add))
                then(nc.vector.tensor_scalar(eden[:, :, :], ed[:, :, :], 1.0, None, ALU.add))
                then(tt(eden[:, :, :], eden[:, :, :], gsum[:, :, :], ALU.mult))
                then(nc.vector.reciprocal(wk[0][:, :, :], eden[:, :, :]))
                then(tt(wk[1][:, :, :], wk[0][:, :, :], ed[:, :, :], ALU.mult))
                dve.wait_ge(S("counts"), L + 1)
                then(nc.vector.tensor_copy(cnt[:, :], bank[1][:, 0:E]))
                then(nc.vector.tensor_tensor_scan(endc[:, :], ones[:, 0:E], cnt[:, :], 0.0, ALU.mult, ALU.add))
                then(tt(offc[:, :], endc[:, :], cnt[:, :], ALU.subtract))
                nc.vector.tensor_copy(off_i[:, L, :], offc[0:1, :]).then_inc(S("off_ready"), 1)
                then(tt(posn[:, :, :], bank[1][:, E:3 * E].rearrange("p (t n) -> p t n", t=T),
                        offc[:, :].unsqueeze(1).broadcast_to([P, T, E]), ALU.add))
                for i in range(2):
                    then(tt(msk[i][:, :, :], msk[i][:, :, :], posn[:, :, :], ALU.mult))
                    then(nc.vector.tensor_reduce(slot_of[i][:, :, :], msk[i][:, :, :], AX, ALU.add))
                for t in range(T):
                    then(nc.vector.tensor_scalar(pick[:, t, :], iota, slot_of[0][:, t, :], None, ALU.is_equal))
                    stt(pick[:, t, :], iota, slot_of[1][:, t, :], pick[:, t, :], ALU.is_equal, ALU.add)\
                        .then_inc(S("pick_ready"), 1)
                if L == 0:
                    dve.wait_ge(S("rw_ready"), 2)
                for t in range(T):
                    tmp = reg_c[:, 1024:1024 + NSLOT]
                    then(nc.vector.tensor_scalar(pickw[:, t, :], iota, slot_of[0][:, t, :], wk[0][:, t, :],
                                                 ALU.is_equal, ALU.mult))
                    then(nc.vector.tensor_scalar(tmp, iota, slot_of[1][:, t, :], wk[1][:, t, :],
                                                 ALU.is_equal, ALU.mult))
                    tt(pickw[:, t, :], pickw[:, t, :], tmp, ALU.add).then_inc(S("pickw_ready"), 1)
                    dve.wait_ge(S("pickw_ready"), L * T + t + 1)
                nc.vector.memset(hS[:, :, NSLOT:PAD], 0.0).then_inc(S("hS_pad"), 1)
                overflow_list()
                ins = nc.vector.tensor_copy(ov_i[:, L, :], ov_f[:, :])
                ins.then_inc(S("ovf_ready"), 1)

            def overflow_list():
                n1, end1, off1 = cnt[0:1, :], endc[0:1, :], offc[0:1, :]
                for q in range(NC_):
                    then(nc.vector.tensor_scalar(ov_ind[:, q, :], n1, float(CAP * (q + 1)), None, ALU.is_gt))
                then(nc.vector.tensor_reduce(ov_n[:, :], ov_ind[:, :, :].rearrange("p q e -> p e q"), AX, ALU.add))
                then(nc.vector.tensor_tensor_scan(ov_end[:, :], ones[0:1, 0:E], ov_n[:, :], 0.0, ALU.mult, ALU.add))
                then(tt(ov_n[:, :], ov_end[:, :], ov_n[:, :], ALU.subtract))
                then(nc.vector.tensor_scalar(ov_last[:, :], end1, -float(CAP), None, ALU.add))
                for q in range(NC_):
                    then(nc.vector.tensor_scalar(ov_rank[:, q, :], ov_n[:, :], float(q), None, ALU.add))
                    then(stt(ov_start[:, q, :], off1, float(CAP * (q + 1)), ov_last[:, :], ALU.add, ALU.min))
                for i in range(MAXOVF):
                    then(stt(ov_tmp[:, :, :], ov_rank[:, :, :], float(i), ov_ind[:, :, :], ALU.is_equal, ALU.mult))
                    then(nc.vector.tensor_tensor_reduce(
                        ov_dump[:, :, :], ov_tmp[:, :, :], iota[0:1, 0:E].unsqueeze(1).broadcast_to([1, NC_, E]),
                        1.0, 0.0, ALU.mult, ALU.add, ov_f[:, i:i + 1]))
                    then(nc.vector.tensor_tensor_reduce(
                        ov_dump[:, :, :], ov_tmp[:, :, :], ov_start[:, :, :],
                        1.0, 0.0, ALU.mult, ALU.add, ov_f[:, MAXOVF + i:MAXOVF + i + 1]))
                then(nc.vector.tensor_copy(ov_f[:, 2 * MAXOVF:2 * MAXOVF + 1], ov_end[:, E - 1:E]))
                ok = ov_n[:, 0:1]
                then(nc.vector.tensor_scalar(ok, ov_end[:, E - 1:E], 0.5, None, ALU.is_lt))
                for s, e in enumerate(STAGES):
                    n = 2 * MAXOVF + 1 + s
                    then(stt(ov_f[:, n:n + 1], offc[0:1, e:e + 1], float((s + 1) * P), ok, ALU.is_ge, ALU.mult))
                    ok = ov_f[:, n:n + 1]

            def expert(L, e, b, s):
                dve.wait_ge(S("gu_ready", L), e + 1)
                dve.wait_ge(S("sil_ready", L), e + 1)
                tt(he[:, b, :], sil[:, b, :], bank[b][:, P:2 * P], ALU.mult).then_inc(S("he_ready", L), 1)
                dve.wait_ge(S("he_turned", L), e + 1)
                nc.vector.tensor_copy(heT[:, b, :], bank[b][:, 2 * P:3 * P]).then_inc(S("heT_ready", L), 1)
                dve.wait_ge(S("dn_ready", L), e + 1)
                dve.sem_inc(S("ring_free", s), 1)
                nc.vector.tensor_copy(ye[:, b, :], bank[2 + b][:, :]).then_inc(S("ye_ready", L), 1)

            def experts(L, e0, e1):
                n0 = IT_EXP[L](e0)
                with dve.Fori(0, (e1 - e0) // R) as i:
                    for u in range(R):
                        expert(L, i * R + (e0 + u), u % 2, (n0 + u) % R)

            def expert_at(L, e):
                expert(L, e, e % 2, IT_EXP[L](e) % R)

            def overflow(L):
                n_ovf = dve.value_load(ov_i[0:1, L, 2 * MAXOVF:2 * MAXOVF + 1], min_val=0, max_val=MAXOVF)
                with dve.If(n_ovf > 0):
                    with dve.Fori(0, n_ovf) as i:
                        dve.wait_ge(S("ovf_sil", L), i + 1)
                        tt(he[:, 0, :], sil[:, 0, :], bank[0][:, P:2 * P], ALU.mult).then_inc(S("ovf_he", L), 1)
                        dve.wait_ge(S("ovf_he_turned", L), i + 1)
                        nc.vector.tensor_copy(heT[:, 0, :], bank[0][:, 2 * P:3 * P]).then_inc(S("ovf_heT", L), 1)
                        dve.wait_ge(S("ovf_pe", L), i * 3 + 4)
                        nc.vector.tensor_copy(ye[:, 0, :], bank[2][:, :]).then_inc(S("ovf_ye", L), 1)

            def evac_yT(L, s):
                dve.wait_ge(S("yT_turned", L), 2 * s + 2)
                nc.vector.tensor_copy(yS[s][:, 512:D], bank[1][:, :]).then_inc(S("yS_dve", L), 1)

            def later_experts(L):
                experts(L, R, STAGES[0])
                for s, e in enumerate(STAGES):
                    expert_at(L, e)
                    with dve.If(flag(dve, L, s) > 0):
                        evac_yT(L, s)
                    for u in range(1, R):
                        expert_at(L, e + u)
                with dve.If(flag(dve, L, SB - 2) < 1):
                    overflow(L)
                    for s in range(SB - 1):
                        with dve.If(flag(dve, L, s) < 1):
                            evac_yT(L, s)
                evac_yT(L, SB - 1)

            for t in range(T):
                reciprocals(0, t)
            norm_mix()
            for b in range(2):
                dve.wait_ge(S("gain_ps"), b + 1)
                cols = slice(2 * D + b * 512, 2 * D + b * 512 + 512)
                tt(mod[:, cols], mod[:, cols], bank[6 + b][:, :], ALU.mult).then_inc(S("ps_used"), 1)
            dve.wait_ge(S("ps_used"), 2)
            add_to_x(S("mix_out", 0), sub_layer(0, "ffn"), 2, reg_b[:, 0:512], 0, lambda t: reciprocals(nth(0, "ffn"), t))
            columns(0, bank[4])
            for t in range(T):
                evac_hT(0, "ffn", t)
            route(0)
            for e in range(R):
                expert_at(0, e)
            columns(1, bank[6])
            later_experts(0)
            add_to_x(S("moe_out", 0), sub_layer(1, "mix"), 5, reg_c[:, 1024:1536], 4, norm_step(1, "mix"))

            for a in range(12, 16):
                ada(a)

            def front(m):
                if m >= 2:
                    dve.wait_ge(S("pT_turned"), 2 * m - 2)
                for a in range(2):
                    hd = 2 * m + a
                    dve.wait_ge(S("s_full"), hd + 1)
                    stt(sc[m % 2][a], alibi, slopes[:, hd:hd + 1], bank[1 + 2 * (m % 2) + a][:, 0:3 * P],
                        ALU.mult, ALU.add).then_inc(S("s_read"), 1)
                    dve.wait_ge(S("s_read"), hd + 1)
                    for t in range(T):
                        nc.vector.tensor_reduce(nmx[:, m % 2, a, t:t + 1], sc[m % 2][a][:, t * P:t * P + (t + 1) * P],
                                                AX, ALU.max, negate=True).then_inc(S("mx_ready"), 1)

            def back(m):
                for a in range(2):
                    dve.wait_ge(S("exp_done"), 4 * m + 2 * a + 2)
                    then(nc.vector.reciprocal(prc[:, m % 2, a, :], psm[:, m % 2, a, :]))
                    for t in range(T):
                        p = sc[m % 2][a][:, t * P:t * P + (t + 1) * P]
                        nc.vector.tensor_scalar(p, p, prc[:, m % 2, a, t:t + 1], None, ALU.mult)\
                            .then_inc(S("p_ready"), 1)

            for m in range(NH // 2):
                if m == 3:
                    dve.wait_ge(S("s_full"), 2 * m + 1)
                    columns(2, bank[3][:, 3 * P:4 * P])
                front(m)
                back(m)
            add_to_x(S("mix_out", 1), sub_layer(1, "ffn"), 2, reg_a[:, 4096:4608], 0, norm_step(1, "ffn"))
            route(1)
            for e in range(R):
                expert_at(1, e)
            later_experts(1)

            def final(t):
                reciprocals(nth(2, "fin"), t)
                dve.wait_ge(S("rs_ready"), nth(2, "fin") * T + t + 1)
                for b in range(2):
                    dve.wait_ge(S("gain_kept"), b + 1)
                    cols = slice(b * 512, b * 512 + 512)
                    stt(h_of[4][:, t, cols], x_sb[:, t, cols], rs[:, t:t + 1], mod[:, cols], ALU.mult, ALU.mult)\
                        .then_inc(S("result_ready"), 1)

            add_to_x(S("moe_out", 1), sub_layer(2, "fin"), 5, reg_c[:, 1024:1536], 4, final)


_INS = ["x", "c", "ada_w", "ada_b", "norm_mix_g", "norm_ffn_g", "pool_w", "pool_scale", "w_qkv", "w_o",
        "router_group_w", "router_expert_w", "exp_w_gate", "exp_w_up", "exp_w_down", "final_norm_g"]


def kernel(**inputs):
    import numpy as _np
    import concourse.bacc as _bacc
    from concourse import mybir as _mybir
    from concourse.bass_utils import run_bass_kernel_spmd as _run

    nc = _bacc.Bacc("TRN2", target_bir_lowering=False, num_devices=1)
    arrays, args = {}, {}
    for name, a in [(n, inputs[n]) for n in _INS] + list(constants().items()):
        a = _np.ascontiguousarray(a)
        arrays[f"in_{name}_dram"] = a
        args[name] = nc.dram_tensor(f"in_{name}_dram", a.shape, _mybir.dt.from_np(a.dtype), kind="ExternalInput").ap()
    out = nc.dram_tensor("out_0_dram", (1, SEQ, D), _mybir.dt.float32, kind="ExternalOutput").ap()
    program(nc, **args, out=out)
    r = _run(nc, [arrays], core_ids=[0])
    return r.results[0]["out_0_dram"]
```
